# Optimizing a Trainium2 kernel written in Bass

```python
import math
import jax, jax.numpy as jnp
from jax import lax
import numpy as np

D_MODEL = 1024
BATCH = 1
SEQ = 256
DEPTH = 2

M_HEADS = 4
M_HEAD_DIM = 128
M_WIDTH = M_HEADS * M_HEAD_DIM
M_CONV = 4
M_CHUNK = 128
M_INIT = -1e30
ROPE_DIM = 64
ROPE_THETA = 10000.0
S_HEADS = 8
S_HEAD_DIM = ROPE_DIM
S_WIDTH = S_HEADS * S_HEAD_DIM
S_KV_RANK = 256
IDX_HEADS = 4
IDX_DIM = ROPE_DIM
IDX_TOPK_MAX = 256
S_QBLOCK = 64
DA_HEADS = 4
DA_HEAD_DIM = ROPE_DIM
DA_V_DIM = 2 * DA_HEAD_DIM
DA_WIDTH = DA_HEADS * DA_V_DIM
DA_QBLOCK = 128
N_BRANCH = 3
BRANCH_WIDTH = 512
FF_DIM = ((8 * D_MODEL + 3 * 256 - 1) // (3 * 256)) * 256
EPS = 1e-6

_SEG_SIZES = (
    2 * M_WIDTH,
    M_WIDTH,
    M_WIDTH,
    2 * M_HEADS,
    S_WIDTH,
    S_KV_RANK,
    IDX_HEADS * IDX_DIM,
    IDX_DIM,
    IDX_HEADS,
    2 * DA_HEADS * DA_HEAD_DIM,
    2 * DA_HEADS * DA_HEAD_DIM,
    DA_WIDTH,
    N_BRANCH * D_MODEL,
)
IN_COLS = sum(_SEG_SIZES)


def _split_cols(z):
    offs = []
    acc = 0
    for s in _SEG_SIZES[:-1]:
        acc += s
        offs.append(acc)
    return jnp.split(z, offs, axis=-1)

def _rms(x, g):
    xf = x.astype(jnp.float32)
    y = xf * lax.rsqrt(jnp.mean(xf * xf, axis=-1, keepdims=True) + EPS)
    return (y * g.astype(jnp.float32)).astype(x.dtype)

def _rope_tables(seq, dim, dtype):
    inv = 1.0 / jnp.power(ROPE_THETA, jnp.arange(0, dim, 2, dtype=jnp.float32) / dim)
    ang = jnp.arange(seq, dtype=jnp.float32)[:, None] * inv[None, :]
    return jnp.cos(ang).astype(dtype), jnp.sin(ang).astype(dtype)

def _rope(x, cos, sin):
    half = x.shape[-1] // 2
    shape = (1, cos.shape[0]) + (1,) * (x.ndim - 3) + (half,)
    c = cos.reshape(shape)
    s = sin.reshape(shape)
    x1, x2 = x[..., :half], x[..., half:]
    return jnp.concatenate([x1 * c - x2 * s, x1 * s + x2 * c], axis=-1)

def _causal_conv(x, w, b):
    k, c = w.shape
    y = lax.conv_general_dilated(x, w[:, None, :], window_strides=(1,), padding=[(k - 1, 0)],
                                 dimension_numbers=('NWC', 'WIO', 'NWC'), feature_group_count=c)
    return y + b

def _mlstm(q, k, v, i_pre, f_pre):
    B, T, H, dh = q.shape
    L = M_CHUNK
    N = T // L
    f32 = jnp.float32

    def chunk(a):
        a = a.astype(f32).reshape((B, N, L, H) + a.shape[3:])
        return jnp.moveaxis(a, 3, 1)

    qc = chunk(q)
    kc = chunk(k) * (dh ** -0.5)
    vc = chunk(v)
    ic = chunk(i_pre)
    lf = jax.nn.log_sigmoid(chunk(f_pre))
    b = jnp.cumsum(lf, axis=-1)
    g = b[..., -1]

    a = g[..., None] - b + ic
    m_loc = a.max(axis=-1)
    w_loc = jnp.exp(a - m_loc[..., None])
    c_loc = jnp.einsum('bhnlv,bhnlk->bhnvk', vc * w_loc[..., None], kc)
    n_loc = jnp.einsum('bhnl,bhnlk->bhnk', w_loc, kc)

    def step(state, xs):
        c_st, n_st, m_st = state
        g_n, c_n, nn_n, m_n = xs
        m_new = jnp.maximum(g_n + m_st, m_n)
        s_old = jnp.exp(g_n + m_st - m_new)
        s_loc = jnp.exp(m_n - m_new)
        c_new = s_old[..., None, None] * c_st + s_loc[..., None, None] * c_n
        n_new = s_old[..., None] * n_st + s_loc[..., None] * nn_n
        return (c_new, n_new, m_new), (c_st, n_st, m_st)

    init = (jnp.zeros((B, H, dh, dh), f32), jnp.zeros((B, H, dh), f32), jnp.full((B, H), M_INIT, f32))
    xs = (jnp.moveaxis(g, 2, 0), jnp.moveaxis(c_loc, 2, 0), jnp.moveaxis(n_loc, 2, 0), jnp.moveaxis(m_loc, 2, 0))
    _, (c_prev, n_prev, m_prev) = lax.scan(step, init, xs)
    c_prev = jnp.moveaxis(c_prev, 0, 2)
    n_prev = jnp.moveaxis(n_prev, 0, 2)
    m_prev = jnp.moveaxis(m_prev, 0, 2)

    t_idx = jnp.arange(L)
    causal = t_idx[:, None] >= t_idx[None, :]
    dmat = b[..., :, None] - b[..., None, :] + ic[..., None, :]
    dmat = jnp.where(causal, dmat, -jnp.inf)
    inter = b + m_prev[..., None]
    m_t = jnp.maximum(inter, dmat.max(axis=-1))
    sw = jnp.exp(dmat - m_t[..., None]) * jnp.einsum('bhntk,bhnsk->bhnts', qc, kc)
    s_inter = jnp.exp(inter - m_t)
    num = jnp.einsum('bhnts,bhnsv->bhntv', sw, vc) + s_inter[..., None] * jnp.einsum('bhntk,bhnvk->bhntv', qc, c_prev)
    den = sw.sum(axis=-1) + s_inter * jnp.einsum('bhntk,bhnk->bhnt', qc, n_prev)
    h = num / jnp.maximum(jnp.abs(den), jnp.exp(-m_t))[..., None]
    return jnp.moveaxis(h, 1, 3).reshape(B, T, H, dh)

def _dsa(q, k, v, qi, ki, wi):
    B, T, H, dh = q.shape
    topk = min(IDX_TOPK_MAX, T // 4)
    nb = T // S_QBLOCK
    f32 = jnp.float32
    bidx = jnp.arange(B)[:, None, None]
    ki32 = ki.astype(f32)
    key_pos = jnp.arange(T)
    idx_scale = (IDX_HEADS * IDX_DIM) ** -0.5

    def blocks(a):
        return jnp.moveaxis(a.reshape((B, nb, S_QBLOCK) + a.shape[2:]), 1, 0)

    def blk(args):
        qb, qib, wib, start = args
        tq = start + jnp.arange(S_QBLOCK)
        causal = key_pos[None, :] <= tq[:, None]
        rel = jax.nn.relu(jnp.einsum('bqhd,bsd->bqhs', qib.astype(f32), ki32))
        score = jnp.einsum('bqh,bqhs->bqs', wib.astype(f32) * idx_scale, rel)
        score = jnp.where(causal[None], score, -jnp.inf)
        _, idx = lax.top_k(score, topk)
        valid = idx <= tq[None, :, None]
        k_sel = k[bidx, idx]
        v_sel = v[bidx, idx]
        s = jnp.einsum('bqhd,bqkhd->bhqk', qb, k_sel).astype(f32) * (dh ** -0.5)
        s = jnp.where(valid[:, None], s, -jnp.inf)
        p = jax.nn.softmax(s, axis=-1).astype(v.dtype)
        return jnp.einsum('bhqk,bqkhd->bqhd', p, v_sel)

    starts = jnp.arange(nb, dtype=jnp.int32) * S_QBLOCK
    out = lax.map(blk, (blocks(q), blocks(qi), blocks(wi), starts))
    return jnp.moveaxis(out, 0, 1).reshape(B, T, H, dh)

def _diff_attn(q, k, v, lam):
    B, T, H, _, d = q.shape
    nb = T // DA_QBLOCK
    f32 = jnp.float32
    key_pos = jnp.arange(T)

    def blk(args):
        qb, start = args
        tq = start + jnp.arange(DA_QBLOCK)
        causal = key_pos[None, :] <= tq[:, None]
        s = jnp.einsum('bqhcd,bshcd->bhcqs', qb, k).astype(f32) * (d ** -0.5)
        s = jnp.where(causal, s, -jnp.inf)
        p = jax.nn.softmax(s, axis=-1)
        a = p[:, :, 0] - lam * p[:, :, 1]
        return jnp.einsum('bhqs,bshv->bqhv', a.astype(v.dtype), v)

    qblk = jnp.moveaxis(q.reshape((B, nb, DA_QBLOCK) + q.shape[2:]), 1, 0)
    starts = jnp.arange(nb, dtype=jnp.int32) * DA_QBLOCK
    out = lax.map(blk, (qblk, starts))
    return jnp.moveaxis(out, 0, 1).reshape(B, T, H, v.shape[-1])

def _layer(x, li, cos, sin, norm_mix_g, w_in, b_gate, conv_w, conv_b, gate_b, m_norm_g,
           kv_norm_g, w_kv_up, sq_g, sk_g, dq_g, dk_g, lam, d_out_g, w_branch, w_out,
           norm_ffn_g, w_gate_up, w_down):
    B, T, _ = x.shape
    f32 = jnp.float32
    xn = _rms(x, norm_mix_g)
    z = jnp.einsum('btd,dc->btc', xn, w_in)
    (m_qk, m_v, m_o, m_if, s_q, s_ckv, i_q, i_k, i_w, d_q, d_k, d_v, g_pre) = _split_cols(z)

    m_qk = jax.nn.silu(_causal_conv(m_qk, conv_w, conv_b))
    mq, mk = jnp.split(m_qk, 2, axis=-1)
    m_if = m_if + gate_b
    h = _mlstm(mq.reshape(B, T, M_HEADS, M_HEAD_DIM), mk.reshape(B, T, M_HEADS, M_HEAD_DIM),
               m_v.reshape(B, T, M_HEADS, M_HEAD_DIM), m_if[..., :M_HEADS], m_if[..., M_HEADS:])
    h = _rms(h, m_norm_g).reshape(B, T, M_WIDTH)
    y_a = (jax.nn.sigmoid(m_o.astype(f32)) * h).astype(x.dtype)

    sq = _rope(_rms(s_q.reshape(B, T, S_HEADS, S_HEAD_DIM), sq_g), cos, sin)
    ckv = _rms(s_ckv, kv_norm_g)
    kv = jnp.einsum('btr,rc->btc', ckv, w_kv_up).reshape(B, T, 2, S_HEADS, S_HEAD_DIM)
    sk = _rope(_rms(kv[:, :, 0], sk_g), cos, sin)
    sv = kv[:, :, 1]
    iq = _rope(i_q.reshape(B, T, IDX_HEADS, IDX_DIM), cos, sin)
    ik = _rope(i_k, cos, sin)
    y_b = _dsa(sq, sk, sv, iq, ik, i_w).reshape(B, T, S_WIDTH)

    dq = _rope(_rms(d_q.reshape(B, T, DA_HEADS, 2, DA_HEAD_DIM), dq_g), cos, sin)
    dk = _rope(_rms(d_k.reshape(B, T, DA_HEADS, 2, DA_HEAD_DIM), dk_g), cos, sin)
    dv = d_v.reshape(B, T, DA_HEADS, DA_V_DIM)
    lamf = lam.astype(f32)
    lam_init = 0.8 - 0.6 * math.exp(-0.3 * li)
    lam_val = jnp.exp(jnp.sum(lamf[0] * lamf[1])) - jnp.exp(jnp.sum(lamf[2] * lamf[3])) + lam_init
    o = _diff_attn(dq, dk, dv, lam_val)
    y_c = (_rms(o, d_out_g) * (1.0 - lam_init)).reshape(B, T, DA_WIDTH)

    gates = jax.nn.sigmoid((g_pre + b_gate).astype(f32)).astype(x.dtype).reshape(B, T, N_BRANCH, D_MODEL)
    merged = (gates[:, :, 0] * jnp.einsum('btc,cd->btd', y_a, w_branch[0])
              + gates[:, :, 1] * jnp.einsum('btc,cd->btd', y_b, w_branch[1])
              + gates[:, :, 2] * jnp.einsum('btc,cd->btd', y_c, w_branch[2]))
    x = x + jnp.einsum('btd,de->bte', merged, w_out)

    xn = _rms(x, norm_ffn_g)
    gu = jnp.einsum('btd,df->btf', xn, w_gate_up)
    g, u = jnp.split(gu, 2, axis=-1)
    return x + jnp.einsum('btf,fd->btd', jax.nn.silu(g) * u, w_down)

def first_inputs(seed: int = 0) -> dict:
    key = jax.random.key(seed)
    ks = jax.random.split(key, 24)
    nrm = jax.random.normal
    f32 = jnp.float32

    def gain(k, shape):
        return 1.0 + 0.02 * nrm(k, shape, f32)

    i_bias = 0.1 * nrm(ks[6], (DEPTH, M_HEADS), f32)
    f_bias = jnp.linspace(3.0, 6.0, M_HEADS, dtype=f32)[None, :] + 0.1 * nrm(ks[7], (DEPTH, M_HEADS), f32)
    return {
        'x': nrm(ks[0], (BATCH, SEQ, D_MODEL), f32),
        'norm_mix_g': gain(ks[1], (DEPTH, D_MODEL)),
        'w_in': nrm(ks[2], (DEPTH, D_MODEL, IN_COLS), f32) * D_MODEL ** -0.5,
        'b_gate': 0.02 * nrm(ks[3], (DEPTH, N_BRANCH * D_MODEL), f32),
        'mlstm_conv_w': nrm(ks[4], (DEPTH, M_CONV, 2 * M_WIDTH), f32) * M_CONV ** -0.5,
        'mlstm_conv_b': 0.02 * nrm(ks[5], (DEPTH, 2 * M_WIDTH), f32),
        'mlstm_gate_b': jnp.concatenate([i_bias, f_bias], axis=-1),
        'mlstm_norm_g': gain(ks[8], (DEPTH, M_HEADS, M_HEAD_DIM)),
        'dsa_kv_norm_g': gain(ks[9], (DEPTH, S_KV_RANK)),
        'dsa_w_kv_up': nrm(ks[10], (DEPTH, S_KV_RANK, 2 * S_WIDTH), f32) * S_KV_RANK ** -0.5,
        'dsa_q_norm_g': gain(ks[11], (DEPTH, S_HEAD_DIM)),
        'dsa_k_norm_g': gain(ks[12], (DEPTH, S_HEAD_DIM)),
        'diff_q_norm_g': gain(ks[13], (DEPTH, DA_HEAD_DIM)),
        'diff_k_norm_g': gain(ks[14], (DEPTH, DA_HEAD_DIM)),
        'diff_lambda': 0.1 * nrm(ks[15], (DEPTH, 4, DA_HEAD_DIM), f32),
        'diff_out_norm_g': gain(ks[16], (DEPTH, DA_V_DIM)),
        'w_branch': nrm(ks[17], (DEPTH, N_BRANCH, BRANCH_WIDTH, D_MODEL), f32) * BRANCH_WIDTH ** -0.5,
        'w_out': nrm(ks[18], (DEPTH, D_MODEL, D_MODEL), f32) * D_MODEL ** -0.5,
        'norm_ffn_g': gain(ks[19], (DEPTH, D_MODEL)),
        'w_gate_up': nrm(ks[20], (DEPTH, D_MODEL, 2 * FF_DIM), f32) * D_MODEL ** -0.5,
        'w_down': nrm(ks[21], (DEPTH, FF_DIM, D_MODEL), f32) * FF_DIM ** -0.5,
    }

def first_block(x, norm_mix_g, w_in, b_gate, mlstm_conv_w, mlstm_conv_b, mlstm_gate_b, mlstm_norm_g,
              dsa_kv_norm_g, dsa_w_kv_up, dsa_q_norm_g, dsa_k_norm_g, diff_q_norm_g, diff_k_norm_g,
              diff_lambda, diff_out_norm_g, w_branch, w_out, norm_ffn_g, w_gate_up, w_down):
    cos, sin = _rope_tables(x.shape[1], ROPE_DIM, x.dtype)
    for li in range(DEPTH):
        x = _layer(x, li, cos, sin, norm_mix_g[li], w_in[li], b_gate[li], mlstm_conv_w[li],
                   mlstm_conv_b[li], mlstm_gate_b[li], mlstm_norm_g[li], dsa_kv_norm_g[li],
                   dsa_w_kv_up[li], dsa_q_norm_g[li], dsa_k_norm_g[li], diff_q_norm_g[li],
                   diff_k_norm_g[li], diff_lambda[li], diff_out_norm_g[li], w_branch[li], w_out[li],
                   norm_ffn_g[li], w_gate_up[li], w_down[li])
    return x


RET_HEADS = 4
RET_QK_DIM = D_MODEL // RET_HEADS
RET_V_DIM = 2 * RET_QK_DIM
RET_QK_TOTAL = RET_HEADS * RET_QK_DIM
RET_V_TOTAL = RET_HEADS * RET_V_DIM
RET_IN_COLS = 2 * RET_QK_TOTAL + 2 * RET_V_TOTAL
RET_CHUNK = 128
ROPE_BASE = 10000.0
CONV_WIDTH = 3
D_FF = 7 * D_MODEL // 2
N_EXPERTS = 8
TOP_K = 2
NORM_EPS = 1e-6


def _rmsnorm(x, g):
    xf = x.astype(jnp.float32)
    y = xf * lax.rsqrt(jnp.mean(xf * xf, axis=-1, keepdims=True) + NORM_EPS)
    return (y * g.astype(jnp.float32)).astype(x.dtype)

def _rotary(t, pos):
    d = t.shape[-1]
    inv_freq = ROPE_BASE ** (-jnp.arange(0, d, 2, dtype=jnp.float32) / d)
    ang = pos[:, None] * inv_freq[None, :]
    cos = jnp.cos(ang)[None, :, None, :]
    sin = jnp.sin(ang)[None, :, None, :]
    t1, t2 = t[..., : d // 2], t[..., d // 2:]
    return jnp.concatenate([t1 * cos - t2 * sin, t1 * sin + t2 * cos], axis=-1)

def _retention(xn, w_in, w_out):
    b, s, _ = xn.shape
    proj = (xn @ w_in).astype(jnp.float32)
    q = proj[..., :RET_QK_TOTAL].reshape(b, s, RET_HEADS, RET_QK_DIM)
    k = proj[..., RET_QK_TOTAL:2 * RET_QK_TOTAL].reshape(b, s, RET_HEADS, RET_QK_DIM)
    v = proj[..., 2 * RET_QK_TOTAL:2 * RET_QK_TOTAL + RET_V_TOTAL].reshape(b, s, RET_HEADS, RET_V_DIM)
    g = proj[..., 2 * RET_QK_TOTAL + RET_V_TOTAL:]
    pos = jnp.arange(s, dtype=jnp.float32)
    q = _rotary(q, pos)
    k = _rotary(k, pos) * (RET_QK_DIM ** -0.5)

    nc = s // RET_CHUNK

    def to_chunks(t):
        return t.reshape(b, nc, RET_CHUNK, RET_HEADS, t.shape[-1]).transpose(1, 0, 3, 2, 4)

    qc, kc, vc = to_chunks(q), to_chunks(k), to_chunks(v)

    log_gamma = jnp.log(1.0 - 2.0 ** (-5.0 - jnp.arange(RET_HEADS, dtype=jnp.float32)))
    idx = jnp.arange(RET_CHUNK, dtype=jnp.float32)
    diff = idx[:, None] - idx[None, :]
    causal = diff >= 0
    intra_decay = jnp.where(causal[None], jnp.exp(jnp.where(causal, diff, 0.0)[None] * log_gamma[:, None, None]), 0.0)
    q_decay = jnp.exp((idx[None, :] + 1.0) * log_gamma[:, None])
    k_decay = jnp.exp((RET_CHUNK - 1.0 - idx[None, :]) * log_gamma[:, None])
    chunk_decay = jnp.exp(RET_CHUNK * log_gamma)

    def step(state, inp):
        q_i, k_i, v_i = inp
        scores = jnp.einsum('bhid,bhjd->bhij', q_i, k_i) * intra_decay[None]
        inner = jnp.einsum('bhij,bhje->bhie', scores, v_i)
        cross = jnp.einsum('bhid,bhde->bhie', q_i * q_decay[None, :, :, None], state)
        new_state = state * chunk_decay[None, :, None, None] + jnp.einsum(
            'bhjd,bhje->bhde', k_i * k_decay[None, :, :, None], v_i)
        return new_state, inner + cross

    state0 = jnp.zeros((b, RET_HEADS, RET_QK_DIM, RET_V_DIM), jnp.float32)
    _, o = lax.scan(step, state0, (qc, kc, vc))
    o = o.transpose(1, 0, 3, 2, 4).reshape(b, s, RET_HEADS, RET_V_DIM)
    o = o * lax.rsqrt(jnp.mean(o * o, axis=-1, keepdims=True) + NORM_EPS)
    o = jax.nn.silu(g) * o.reshape(b, s, RET_V_TOTAL)
    return o.astype(xn.dtype) @ w_out

def _short_conv(xn, w_in, w_conv, w_out):
    s = xn.shape[1]
    proj = xn @ w_in
    gate_b = proj[..., :D_MODEL]
    gate_c = proj[..., D_MODEL:2 * D_MODEL]
    h = proj[..., 2 * D_MODEL:]
    u = (gate_c * h).astype(jnp.float32)
    u_pad = jnp.pad(u, ((0, 0), (CONV_WIDTH - 1, 0), (0, 0)))
    wc = w_conv.astype(jnp.float32)
    y = sum(wc[j][None, None, :] * u_pad[:, j:j + s, :] for j in range(CONV_WIDTH))
    y = gate_b.astype(jnp.float32) * y
    return y.astype(xn.dtype) @ w_out

def _swiglu(xn, w_gate, w_up, w_down):
    return (jax.nn.silu(xn @ w_gate) * (xn @ w_up)) @ w_down

def _moe_swiglu(xn, w_router, w_gate_e, w_up_e, w_down_e):
    b, s, d = xn.shape
    t = xn.reshape(b * s, d)
    logits = (t @ w_router).astype(jnp.float32)
    top_vals, top_idx = lax.top_k(logits, TOP_K)
    top_w = jax.nn.softmax(top_vals, axis=-1)
    gates = jnp.sum(jax.nn.one_hot(top_idx, N_EXPERTS, dtype=jnp.float32) * top_w[..., None], axis=1)
    out = jnp.zeros((b * s, d), jnp.float32)
    for e in range(N_EXPERTS):
        h = jax.nn.silu(t @ w_gate_e[e]) * (t @ w_up_e[e])
        out = out + gates[:, e:e + 1] * (h @ w_down_e[e]).astype(jnp.float32)
    return out.astype(xn.dtype).reshape(b, s, d)

def second_inputs(seed: int = 0) -> dict:
    key = jax.random.key(seed)
    ks = jax.random.split(key, 24)

    def w(k, shape, fan_in):
        return jax.random.normal(k, shape, jnp.float32) * (fan_in ** -0.5)

    def gain(k):
        return 1.0 + 0.02 * jax.random.normal(k, (D_MODEL,), jnp.float32)

    return {
        "x": jax.random.normal(ks[0], (BATCH, SEQ, D_MODEL), jnp.float32),
        "norm_mix0": gain(ks[1]),
        "ret_w_in": w(ks[2], (D_MODEL, RET_IN_COLS), D_MODEL),
        "ret_w_out": w(ks[3], (RET_V_TOTAL, D_MODEL), RET_V_TOTAL),
        "norm_ffn0": gain(ks[4]),
        "ffn_w_gate": w(ks[5], (D_MODEL, D_FF), D_MODEL),
        "ffn_w_up": w(ks[6], (D_MODEL, D_FF), D_MODEL),
        "ffn_w_down": w(ks[7], (D_FF, D_MODEL), D_FF),
        "norm_mix1": gain(ks[8]),
        "conv_w_in": w(ks[9], (D_MODEL, 3 * D_MODEL), D_MODEL),
        "conv_w": w(ks[10], (CONV_WIDTH, D_MODEL), CONV_WIDTH),
        "conv_w_out": w(ks[11], (D_MODEL, D_MODEL), D_MODEL),
        "norm_ffn1": gain(ks[12]),
        "moe_router": w(ks[13], (D_MODEL, N_EXPERTS), D_MODEL),
        "moe_w_gate": w(ks[14], (N_EXPERTS, D_MODEL, D_FF), D_MODEL),
        "moe_w_up": w(ks[15], (N_EXPERTS, D_MODEL, D_FF), D_MODEL),
        "moe_w_down": w(ks[16], (N_EXPERTS, D_FF, D_MODEL), D_FF),
        "norm_final": gain(ks[17]),
    }

def second_block(x, norm_mix0, ret_w_in, ret_w_out, norm_ffn0, ffn_w_gate, ffn_w_up, ffn_w_down,
              norm_mix1, conv_w_in, conv_w, conv_w_out, norm_ffn1, moe_router, moe_w_gate,
              moe_w_up, moe_w_down, norm_final):
    mixer_params = [(norm_mix0, ret_w_in, ret_w_out), (norm_mix1, conv_w_in, conv_w, conv_w_out)]
    ffn_params = [(norm_ffn0, ffn_w_gate, ffn_w_up, ffn_w_down),
                  (norm_ffn1, moe_router, moe_w_gate, moe_w_up, moe_w_down)]
    h = x
    for i in range(DEPTH):
        mp = mixer_params[i]
        if i % 2 == 0:
            h = h + _retention(_rmsnorm(h, mp[0]), mp[1], mp[2])
        else:
            h = h + _short_conv(_rmsnorm(h, mp[0]), mp[1], mp[2], mp[3])
        fp = ffn_params[i]
        if i % 2 == 0:
            h = h + _swiglu(_rmsnorm(h, fp[0]), fp[1], fp[2], fp[3])
        else:
            h = h + _moe_swiglu(_rmsnorm(h, fp[0]), fp[1], fp[2], fp[3], fp[4])
    return _rmsnorm(h, norm_final)


def setup_inputs(seed=0):
    out = dict(first_inputs(seed))
    for name, value in second_inputs(seed + 1).items():
        if name != "x":
            out[name + "_2"] = value
    return out


def reference(
    x, norm_mix_g, w_in, b_gate, mlstm_conv_w, mlstm_conv_b, mlstm_gate_b, mlstm_norm_g,
    dsa_kv_norm_g, dsa_w_kv_up, dsa_q_norm_g, dsa_k_norm_g, diff_q_norm_g, diff_k_norm_g,
    diff_lambda, diff_out_norm_g, w_branch, w_out, norm_ffn_g, w_gate_up, w_down, norm_mix0_2,
    ret_w_in_2, ret_w_out_2, norm_ffn0_2, ffn_w_gate_2, ffn_w_up_2, ffn_w_down_2, norm_mix1_2,
    conv_w_in_2, conv_w_2, conv_w_out_2, norm_ffn1_2, moe_router_2, moe_w_gate_2, moe_w_up_2,
    moe_w_down_2, norm_final_2,
):
    x = first_block(
        x, norm_mix_g, w_in, b_gate, mlstm_conv_w, mlstm_conv_b, mlstm_gate_b, mlstm_norm_g,
        dsa_kv_norm_g, dsa_w_kv_up, dsa_q_norm_g, dsa_k_norm_g, diff_q_norm_g, diff_k_norm_g,
        diff_lambda, diff_out_norm_g, w_branch, w_out, norm_ffn_g, w_gate_up, w_down,
    )
    return second_block(
        x, norm_mix0_2, ret_w_in_2, ret_w_out_2, norm_ffn0_2, ffn_w_gate_2, ffn_w_up_2,
        ffn_w_down_2, norm_mix1_2, conv_w_in_2, conv_w_2, conv_w_out_2, norm_ffn1_2,
        moe_router_2, moe_w_gate_2, moe_w_up_2, moe_w_down_2, norm_final_2,
    )


_drawn_inputs = setup_inputs


def setup_inputs(seed=0):
    import zlib

    import numpy as np

    out = dict(_drawn_inputs(seed))
    spreads = {}
    factors = {'b_gate': 2.691,
     'dsa_kv_norm_g': 3.349,
     'dsa_q_norm_g': 3.19,
     'dsa_k_norm_g': 8.0,
     'norm_ffn0_2': 3.4,
     'norm_final_2': 22.844,
     'norm_mix0_2': 4.488,
     'norm_mix1_2': 8.0,
     'norm_ffn1_2': 64.0}
    for name, (base, spread) in spreads.items():
        noise = np.random.default_rng([zlib.crc32(name.encode()), seed]).standard_normal(out[name].shape)
        drawn = base * np.exp(spread * noise) if base else spread * noise
        out[name] = __import__('jax').numpy.asarray(drawn.astype(out[name].dtype))
    for name, factor in factors.items():
        out[name] = (out[name] * factor).astype(out[name].dtype)
    return out
```

```python
import math
from contextlib import ExitStack, contextmanager

import numpy as np
import concourse.bass as bass
from concourse import mybir

F32 = mybir.dt.float32
F32R = mybir.dt.float32r
I32 = mybir.dt.int32
ALU = mybir.AluOpType
ACT = mybir.ActivationFunctionType
AX = mybir.AxisListType

P = 128
D = 1024
KT = D // P
SEQ = 256
TT = SEQ // P
DEPTH = 2
HALF = 512
EPS = 1e-6
NEG = -1e30
TAKEN = -3e38

M_HEADS, M_DH = 4, 128
S_HEADS, HD = 8, 64
KV_RANK = 256
IDX_HEADS = 4
TOPK = 64
DA_HEADS = 4
C_QK, C_V, C_O, C_IF = 0, 1024, 1536, 2048
C_SQ, C_CKV, C_IQ, C_IK, C_IW, C_DQ, C_DK, C_DV, C_G = 2056, 2568, 2824, 3080, 3144, 3148, 3660, 4172, 4684
IN_COLS = 7756
FF1 = 2816
RH = 4
D_FF = 3584
NE = 8

UNIT = 2048
RING = 6
SPLITS = 4
PARAMS = 24
EXPERT_UNITS = 3 * D * D_FF // (P * UNIT)
EXPERT_SPLIT = 2 * EXPERT_UNITS // 3
ZF = TT * (IN_COLS - C_O)
ZW = IN_COLS - C_O

K_C2, K_S2, K_ID = 0, 128, 256
K_DIAG = K_ID + P
K_CMT = K_DIAG + P
K_UT = K_CMT + 384
K_ONE = K_UT + P
K_IOTA = K_ONE + P
K_TRI = K_IOTA + 256
K_COLS = K_TRI + NE * NE
K_COSR, K_SINR, K_DECAY = 0, 256, 512
K2_COLS = K_DECAY + RH * 384

G_MIX, G_FFN, G_CB, G_CW, G_MN, G_KV, G_DO = 0, 16, 32, 48, 112, 120, 124
G_ROWS_A = 126
G_MIX0, G_FFN0, G_MIX1, G_FFN1, G_CW2 = 126, 134, 142, 150, 158
G_ROWS = 182


class Signal:

    def __init__(self, name, sem, per_trip=0):
        self.name, self.sem, self.per_trip = name, sem, per_trip
        self.marked, self.seen = 0, {}

    def tick(self, n=1):
        self.marked += n
        return n


class Engine:

    def __init__(self, eng, name, points):
        self.eng, self.name, self.trip = eng, name, None
        self.points, self.at_point = points, {}

    def at(self, sig, value):
        return value if self.trip is None else self.trip * sig.per_trip + value

    def next(self, sig, n=1):
        sig.seen[self.name] = sig.seen.get(self.name, 0) + n
        return self.at(sig, sig.seen[self.name])

    def latest(self, sig):
        return self.at(sig, sig.marked)

    def point(self, name, sig):
        i = self.at_point[name, sig.name] = self.at_point.get((name, sig.name), -1) + 1
        return self.at(sig, self.points[name][i][sig.name])

    @contextmanager
    def trips(self, n, signals):
        before = {s: (s.marked, s.seen.get(self.name, 0)) for s in signals}
        with self.eng.Fori(0, n) as e:
            self.trip = e
            yield e
        self.trip = None
        for s, (marked, seen) in before.items():
            now = s.seen.get(self.name, 0)
            for old, new in ((marked, s.marked), (seen, now)):
                assert new - old in (0, s.per_trip), (s.name, new - old, s.per_trip)
            s.marked += (n - 1) * (s.marked - marked)
            s.seen[self.name] = now + (n - 1) * (now - seen)


def build(nc, a, out):
    ctx = ExitStack()
    with ctx:
        def sb(name, shape, dt=F32):
            return ctx.enter_context(nc.sbuf_tensor(name, shape, dt))

        def signal(name, per_trip=0):
            s = Signal(name, ctx.enter_context(nc.semaphore(name)), per_trip)
            signals.append(s)
            return s

        signals = []
        const = sb("const", [P, K_COLS])
        gcol = sb("gcol", [P, G_ROWS])
        qk_gain = sb("qk_gain", [P, 4, DEPTH, HD])
        gateb = sb("gateb", [M_HEADS, DEPTH * 2])
        bgate = sb("bgate", [DEPTH * 6, HALF])
        w_if = sb("w_if", [P, DEPTH, KT, 8])
        w_rt = sb("w_rt", [P, KT, NE])

        x = sb("x_resid", [P, TT, D])
        xs = sb("xs", [P, TT, D])
        xnT = sb("xnT", [P, KT, SEQ])
        ring = sb("ring", [P, RING, UNIT])

        iqT = sb("iqT", [P, 2, SEQ])
        ikT = sb("ikT", [P, SEQ])
        ckvT = sb("ckvT", [P, 2, SEQ])
        kv = xs
        ybuf = sb("ybuf", [P, 3 * 4 * SEQ])
        yT = ybuf[:, :].rearrange("p (b f t) -> p b f t", b=3, f=4)
        table2 = ybuf[:, 0:K2_COLS]
        fin_g = ybuf[:, K2_COLS:K2_COLS + D]
        tmp = sb("tmp", [P, 4, HALF])
        msel = sb("msel", [P, 384])
        rowf = ybuf[0:M_HEADS, 4 * SEQ:12 * SEQ].rearrange("p (r t) -> p r t", t=SEQ)
        xsum = sb("xsum", [P, 4, TT])
        hsum = sb("hsum", [P, 4, 80])
        kA, kB, kY = 0, 50, 66
        nmax = sb("nmax", [P, 16])
        psum_row = sb("psum_row", [P, 3, 16])
        floor = sb("floor", [P, 4, 8])
        lam = sb("lam", [P, 4, 2 * DEPTH])
        dgain = sb("dgain", [P, DEPTH])
        iw = sb("iw", [P, TT, IDX_HEADS])
        idx = sb("idx", [P, 384])
        work = sb("work", [P, 384])
        cz = sb("causal2", [P, SEQ])
        top8 = sb("top8", [P, 8])
        rt = sb("rt", [P, 12, TT, NE])
        cmp = sb("cmp", [P, 2, NE * NE])
        rt2 = sb("rt2", [P, 6, TT])
        cnt = sb("cnt", [P, NE + 1], I32)
        route = sb("route", [P, 2, TT, NE + 1])

        with ExitStack() as mixers:
            def mx(name, shape):
                return mixers.enter_context(nc.sbuf_tensor(name, shape, F32))

            z = mx("z", [P, ZF])
            v_ext = mx("v_ext", [P, TT, M_HEADS, M_DH + 1])
            CP = KT * (SEQ + 3)
            qkbuf = mx("qkbuf", [P, CP + KT * SEQ])
            cpad = qkbuf[:, 0:CP].rearrange("p (f t) -> p f t", f=KT)
            mqkT = qkbuf[:, CP:CP + KT * SEQ].rearrange("p (f t) -> p f t", f=KT)
            hT4 = qkbuf[:, 0:16 * SEQ].rearrange("p (w f t) -> p w f t", w=4, f=4)
            pbuf = mx("pbuf", [P, 6, HALF])
            grow = pbuf[:, 0, 0:2 * P].rearrange("p (t c) -> p t c", t=2)
            lamv = pbuf[:, 1, :].rearrange("p (l a d) -> p l a d", l=DEPTH, a=4)
            pT = mx("pT", [P, 2, HALF])
            yb = mx("yb", [P, TT, HALF])
        with ExitStack() as ffns:
            def fx(name, shape, dt=F32R):
                return ffns.enter_context(nc.sbuf_tensor(name, shape, dt))

            parts = fx("parts", [P, 2, KT + 4, SEQ])
            split = fx("split", [P, SPLITS, 2, UNIT])

        bank = [ctx.enter_context(nc.psum_tensor(f"bank{i}", [P, HALF], F32)) for i in range(8)]

        zt = z[:, :].rearrange("p (t c) -> p t c", t=TT)

        def zc(tt, col, n):
            return zt[:, tt, col - C_O:col - C_O + n]

        ident = const[:, K_ID:K_ID + P]
        ones = const[:, K_ONE:K_ONE + P]
        qT2 = z[:, 0:4096].rearrange("p (f t) -> p f t", t=SEQ)
        rv = z[:, 4096:8192].rearrange("p (t c) -> p t c", t=TT)
        rg = z[:, 8192:12288].rearrange("p (t c) -> p t c", t=TT)
        oT2 = qT2
        cB = z[:, 0:2048].rearrange("p (f t) -> p f t", t=SEQ)
        cC = z[:, 2048:4096].rearrange("p (f t) -> p f t", t=SEQ)
        upad = z[:, 4096:4096 + KT * (SEQ + 2)].rearrange("p (f t) -> p f t", t=SEQ + 2)
        cyT = z[:, 8192:10240].rearrange("p (f t) -> p f t", t=SEQ)
        pick = table2[:, 0:512].rearrange("p (t s) -> p t s", t=TT)
        pickg = table2[:, 512:1024].rearrange("p (t s) -> p t s", t=TT)
        hT = table2[:, 1024:2048].rearrange("p (t f c) -> p t f c", t=2, f=4)
        putT = ckvT
        ysb = xnT[:, :, :].rearrange("p (s k) t -> p s (k t)", s=2)
        R_LOGIT, R_RANK, R_M0, R_M1, R_TMP, R_MASK, R_GATE, R_SLOT = range(8)
        hb = tmp[:, 0:2, :]
        sg = tmp[:, 2:4, :]

        loaded = [signal(f"weights_loaded{i}", 16 * EXPERT_UNITS // RING) for i in range(RING)]
        params = signal("params_loaded")
        stored = signal("stored")
        GROUPS = D_FF // HALF
        used = signal("weights_used", EXPERT_UNITS - 2 * GROUPS - 1)
        N_ACT = 4 + 3 * GROUPS + 2
        N_DVE = 1 + 3 * GROUPS + 2 + 4
        for_act = signal("bank_for_act", N_ACT)
        for_dve = signal("bank_for_dve", N_DVE)
        act_freed = signal("act_emptied", N_ACT)
        dve_freed = signal("dve_emptied", N_DVE)
        high_made = signal("weights_high")
        high_act = signal("expert_weights_high", EXPERT_SPLIT)
        low_made = signal("weights_low", EXPERT_SPLIT)
        x_low = signal("inputs_low", 4)
        hidden_low = signal("hidden_low")
        act_step = signal("act_step")
        dve_step = signal("dve_step")
        setup_dve = signal("setup_by_dve")
        squares = signal("squares_summed")
        mean_sq = signal("mean_square")
        root = signal("root")
        rstd_dve = signal("rstd")
        xs_act = signal("xs_by_act")
        xs_dve = signal("xs_by_dve")
        conv_dve = signal("conv_done")
        silu_act = signal("mqk_silu")
        absf_dve = signal("forget_abs")
        logf_act = signal("forget_log")
        row_dve = signal("mlstm_rows")
        decay_act = signal("decays")
        floor_act = signal("floor")
        kvn_dve = signal("ckv_normed")
        rope_dve = signal("rope_done")
        score_dve = signal("scores_masked")
        prob_act = signal("probabilities")
        diff_dve = signal("differential_weights")
        yb_dve = signal("branch_token_major")
        sig_act = signal("sigmoids")
        mrg_dve = signal("merged")
        lam_dve = signal("lambda_sums")
        lam_act = signal("lambda_exps")
        ret_dve = signal("retention_rotated")
        rsilu_act = signal("retention_gate")
        rets_dve = signal("retention_scaled")
        conv2_dve = signal("conv2_out")
        mask_dve = signal("routing_mask")
        diff2_dve = signal("routing_difference")
        exp2_act = signal("routing_exp")
        pick_dve = signal("pick_ready", 1)
        late = signal("second_tables_loaded")
        out_dve = signal("output_ready")

        low_banks, unit_of_split = [], []
        act_banks, dve_banks, points, unit_read, split_read = [], [], {}, [], []

        def unit_k(w, col, n, kh):
            return w[kh * HALF:(kh + 1) * HALF, col:col + n].rearrange("(k p) c -> p k c", p=P)

        def unit_r(w, r):
            return w[r * 256:(r + 1) * 256, :].rearrange("(k p) c -> p k c", p=P)

        def place(n, shape):
            k, c = shape
            return ring[:, n % RING, 0:k * c].rearrange("p (k c) -> p k c", k=k)

        gates_after = dict(z=2, kv=2, mlstm=0, dsa=1, diff=1)
        def place_split(m, shape):
            k, c = shape
            return [split[:, m % SPLITS, i, 0:k * c].rearrange("p (k c) -> p k c", k=k) for i in range(2)]

        def group_units(i, groups):
            up = (2 if groups[i][1] == HALF else 1) if i < len(groups) else 0
            return up, groups[i - 1][1] // 256 if i else 0

        z_chunks = [(C_V, 512), (C_O, 512)] + [(C_SQ + 438 * i, 438) for i in range(6)]
        g_chunks = [(C_G + 512 * i, 512) for i in range(6)]
        def score_bank(j):
            return (0, P, range(j, 8, 2)) if j < 2 else (1, SEQ, range(j // 4 * 4 + j % 2, j // 4 * 4 + 4, 2))

        groups1 = [(512 * i, 512) for i in range(5)] + [(2560, 256)]
        groups2 = [(512 * i, 512) for i in range(7)]

        block = ctx.enter_context(nc.Block())

        @block.tensor
        def _(eng):
            pe = Engine(eng, "pe", points)
            issued = [0]
            n_split = [0]
            last = {}
            turn = {}
            last_bank = [None]

            def take(shape):
                n = issued[0]
                issued[0] += 1
                eng.wait_ge(loaded[n % RING].sem, pe.at(loaded[n % RING], 16 * (n // RING + 1)))
                return place(n, shape)

            def take_split(shape):
                issued[0] += 1
                n_split[0] += 1
                unit_of_split.append(issued[0] - 1)
                unit_read.append((low_made, n_split[0]))
                eng.wait_ge(low_made.sem, pe.at(low_made, n_split[0]))
                return place_split(n_split[0] - 1, shape)

            def free_bank(b):
                for sig, token in last.pop(b, []):
                    eng.wait_ge(sig.sem, pe.at(sig, token))

            def fill(pool):
                i = turn.get(pool, 0)
                turn[pool] = i + 1
                b = pool[i % len(pool)]
                free_bank(b)
                return b

            def hand(ins, b, who):
                sig, banks = (for_act, act_banks) if who == "act" else (for_dve, dve_banks)
                ins.then_inc(sig.sem, sig.tick())
                banks.append(b)
                last[b] = [(act_freed if who == "act" else dve_freed, sig.marked)]

            ALL = tuple(range(8))
            LOW = (0, 1, 2, 3)

            def mm(o, l, r, first, final, **kw):
                return nc.tensor.matmul(o, l, r, start=first, stop=final, **kw)

            def point(name):
                points.setdefault(name, []).append(
                    {act_freed.name: for_act.marked, dve_freed.name: for_dve.marked})

            def read(ins, units):
                if ins is not None:
                    ins.then_inc(used.sem, used.tick())
                    unit_read.extend([(used, used.marked)] * units)

            def read_by(sig, units):
                unit_read.extend([(sig, sig.marked)] * units)

            def split_done(sig, units):
                split_read.extend([(sig, sig.marked)] * units)

            def mm3(o, l, r, first, final):
                mm(o, l(0), r(0), first, False)
                mm(o, l(0), r(1), False, False)
                return mm(o, l(1), r(0), False, final)

            def transposes(src_of, n_src, who, pool=ALL, rows=P):
                b = fill(pool)
                for i in range(n_src):
                    ins = nc.tensor.transpose(bank[b][:, i * P:i * P + rows], src_of(i), ident[0:rows, 0:rows])
                hand(ins, b, who)
                last_bank[0] = b

            def norm_transposes():
                eng.wait_ge(xs_act.sem, pe.next(xs_act))
                eng.wait_ge(xs_dve.sem, pe.next(xs_dve))
                for kp in range(4):
                    transposes(lambda i: xs[:, i % 2, (2 * kp + i // 2) * P:(2 * kp + i // 2 + 1) * P], 4,
                               "act" if kp % 2 == 0 else "dve")

            def give_low(b):
                last[b].append((x_low, x_low.marked + x_low.tick()))
                low_banks.append(b)

            def ffn_input():
                eng.wait_ge(xs_act.sem, pe.next(xs_act))
                eng.wait_ge(xs_dve.sem, pe.next(xs_dve))
                for kp in range(4):
                    transposes(lambda i: xs[:, i % 2, (2 * kp + i // 2) * P:(2 * kp + i // 2 + 1) * P], 4, "act")
                    point("input")
                    give_low(last_bank[0])
                eng.wait_ge(x_low.sem, pe.at(x_low, x_low.marked))

            def xnT_wait():
                point("xnT")
                eng.wait_ge(act_freed.sem, pe.point("xnT", act_freed))
                eng.wait_ge(dve_freed.sem, pe.point("xnT", dve_freed))

            def token_major(w_views, n, lhs, ntile, who, pool=ALL, bias=None):
                for tt in range(TT):
                    b = fill(pool)
                    if bias is not None:
                        mm(bank[b][:, 0:n], ident[0:12, bias:bias + 1].broadcast_to([12, P]), bgate[:, 0:n],
                           True, False)
                    for k in range(ntile):
                        w = w_views[k // 4] if ntile == 8 else w_views[k // 2]
                        ins = mm(bank[b][:, 0:n], lhs(k, tt), w[:, k % 4 if ntile == 8 else k % 2, :],
                                 k == 0 and bias is None, k == ntile - 1)
                    hand(ins, b, who(tt))
                return ins

            def xn_tile(k, tt):
                return xnT[:, k, tt * P:(tt + 1) * P]

            def chunk(n, who, bias=None):
                views = [take((4, n)), take((4, n))]
                token_major(views, n, xn_tile, KT, lambda tt: who, bias=bias)
                read_by(for_act, 2)

            def feature_major(who, tiles=4):
                views = [take((4, 512)), take((4, 512))]
                for fp in range(2):
                    b = fill(ALL)
                    for f in range(2):
                        for k in range(KT):
                            c = (2 * fp + f) * P
                            ins = mm(bank[b][:, f * SEQ:(f + 1) * SEQ], views[k // 4][:, k % 4, c:c + P],
                                     xnT[:, k, :], k == 0, k == KT - 1)
                    hand(ins, b, who)
                read_by(for_act if who == "act" else for_dve, 2)

            def to_x(lhs, ntile, units):
                bs = [fill(ALL) for _ in range(4)]
                for u in range(units):
                    w = take((2, 1024))
                    for k in (2 * u, 2 * u + 1):
                        for tt in range(TT):
                            for h in range(2):
                                ins = mm(bank[bs[2 * tt + h]][:, :], lhs(k, tt), w[:, k % 2, h * HALF:(h + 1) * HALF],
                                         k == 0, k == ntile - 1)
                                if k == ntile - 1:
                                    hand(ins, bs[2 * tt + h], "dve")
                    if u < units - 1:
                        read(ins, 1)
                    else:
                        read_by(for_dve, 1)
                point("x")
                point("mixed")

            def ffn(groups, big=None, next_tokens=None):
                dense = big is None
                unit, product, done = (take_split, mm3, split_done) if dense else (take, mm1, read_by)
                part = (lambda w, i: w[i]) if dense else (lambda w, i: w)

                def both(body):
                    if big is None:
                        body(1)
                    else:
                        with eng.If(big):
                            body(1)
                    return body(0)

                def gate_or_up(n, who):
                    b = [fill(LOW), fill(LOW)]
                    shape = (4, 512) if n == 512 else (8, 256)
                    for first in range(0, KT, shape[0]):
                        w = take_split(shape)

                        def body(tt):
                            c = slice(tt * P, (tt + 1) * P)
                            return [mm3(bank[b[tt]][:, 0:n], lambda i: parts[:, i, k, c],
                                        lambda i: w[i][:, k - first, :], k == 0, k == KT - 1)
                                    for k in range(first, first + shape[0])]
                        ins = both(body)
                        if first + shape[0] < KT:
                            ins[-1].then_inc(used.sem, used.tick())
                            split_done(used, 1)
                    hand(ins[0], b[1], who)
                    hand(ins[-1], b[0], who)
                    split_done(for_act if who == "act" else for_dve, 1)
                    point("gate" if who == "act" else "up")

                def turn_hidden(n):
                    eng.wait_ge(dve_freed.sem, pe.point("up", dve_freed))
                    b = [fill(LOW), fill(LOW)]

                    def body(tt):
                        return [nc.tensor.transpose(bank[b[tt]][:, f * P:(f + 1) * P],
                                                    hb[:, tt, f * P:(f + 1) * P], ident) for f in range(n // P)]
                    ins = both(body)
                    hand(ins[0], b[1], "act" if dense else "dve")
                    hand(ins[-1], b[0], "act")
                    point("turned" if dense else "turned for an expert")
                    if dense:
                        for tt in (1, 0):
                            last[b[tt]].append((hidden_low, hidden_low.marked + hidden_low.tick()))
                            low_banks.append(b[tt])

                def down(n, g, ends):
                    if dense:
                        eng.wait_ge(hidden_low.sem, pe.at(hidden_low, hidden_low.marked))
                    else:
                        eng.wait_ge(act_freed.sem, pe.point("turned for an expert", act_freed))
                        eng.wait_ge(dve_freed.sem, pe.point("turned for an expert", dve_freed))
                    for u in range(n // 256):
                        w = unit((2, 1024))

                        def body(tt):
                            c = slice(tt * P, (tt + 1) * P)
                            return [product(bank[4 + 2 * tt + h][:, :], (lambda i: parts[:, i, KT + f, c]) if dense
                                            else (lambda i: hT[:, tt, f, :]),
                                            lambda i: part(w, i)[:, f % 2, h * HALF:(h + 1) * HALF],
                                            g == 0 and f == 0, ends and f == n // P - 1)
                                    for f in (2 * u, 2 * u + 1) for h in range(2)]
                        ins = both(body)
                        if not ends or u < n // 256 - 1:
                            ins[-1].then_inc(used.sem, used.tick())
                            done(used, 1)
                    if ends:
                        first = "dve" if big is None else "act"
                        for i, b, who in ((0, 6, "dve"), (1, 7, "dve"), (2, 4, first), (3, 5, first)):
                            hand(ins[i], b, who)
                        done(for_dve if dense else for_act, 1)

                for b in (4, 5, 6, 7):
                    free_bank(b)
                for i, (_, n) in enumerate(groups):
                    if i:
                        turn_hidden(groups[i - 1][1])
                    gate_or_up(n, "act")
                    gate_or_up(n, "dve")
                    if i:
                        down(groups[i - 1][1], i - 1, False)
                turn_hidden(groups[-1][1])
                if not dense:
                    next_tokens()
                down(groups[-1][1], len(groups) - 1, True)
                point("x" if big is None else "y")

            def mm1(o, l, r, first, final):
                return mm(o, l(0), r(0), first, final)

            eng.wait_ge(params.sem, pe.next(params, 16 * PARAMS))
            b = fill(ALL)
            nc.tensor.transpose(bank[b][:, 0:G_ROWS_A], grow[0:G_ROWS_A, 0, :], ident[0:G_ROWS_A, 0:G_ROWS_A])
            nb = G_ROWS - G_ROWS_A
            ins = nc.tensor.transpose(bank[b][:, G_ROWS_A:G_ROWS], grow[0:nb, 1, :], ident[0:nb, 0:nb])
            hand(ins, b, "dve")

            def layer(li):
                norm_transposes()
                xnT_wait()
                b = fill(ALL)
                for g in range(2):
                    for k in range(KT):
                        ins = mm(bank[b][0:4, g * SEQ:(g + 1) * SEQ], w_if[:, li, k, 4 * g:4 * g + 4], xnT[:, k, :],
                                 k == 0, k == KT - 1)
                hand(ins, b, "dve")
                for _ in range(2):
                    feature_major("act")
                    point("qk")
                for _, n in z_chunks:
                    chunk(n, "act")
                point("z")
                g_left = [list(range(6))]

                def gates(m):
                    for c in range(m):
                        i = g_left[0].pop(0)
                        pe_bias = li * 6 + i
                        chunk(512, "act", bias=pe_bias)

                gates(gates_after["z"])
                eng.wait_ge(kvn_dve.sem, pe.next(kvn_dve))
                transposes(lambda i: yb[:, i % 2, (i // 2) * P:(i // 2 + 1) * P], 4, "dve")
                point("ckvT")
                eng.wait_ge(dve_freed.sem, pe.point("ckvT", dve_freed))
                w = take((2, 1024))
                for tt in range(TT):
                    for h in range(2):
                        b = fill(ALL)
                        for k in range(2):
                            ins = mm(bank[b][:, :], ckvT[:, k, tt * P:(tt + 1) * P], w[:, k, h * HALF:(h + 1) * HALF],
                                     k == 0, k == 1)
                        hand(ins, b, "act")
                read_by(for_act, 1)
                point("kv")
                gates(gates_after["kv"])
                mlstm()
                gates(gates_after["mlstm"])
                eng.wait_ge(rope_dve.sem, pe.next(rope_dve))
                for col in (C_SQ, None, C_DQ, C_DK):
                    for half in range(2):
                        def src(i):
                            c = (2 * half + i // 2) * P
                            return kv[:, i % 2, c:c + P] if col is None else zc(i % 2, col + c, P)
                        transposes(src, 4, "act")
                transposes(lambda i: zc(i % 2, C_IQ + (i // 2) * P, P), 4, "act")
                transposes(lambda i: tmp[:, 3, i * P:(i + 1) * P], 2, "act")
                point("heads")
                eng.wait_ge(act_freed.sem, pe.point("heads", act_freed))
                for tt in range(TT):
                    for odd in range(2):
                        b = fill(ALL)
                        q = slice(64 * odd, 64 * odd + 64)
                        n = (tt + 1) * P
                        for i in range(2):
                            ins = mm(bank[b][:, i * n:(i + 1) * n], iqT[q, i, tt * P:(tt + 1) * P], ikT[q, 0:n],
                                     True, True)
                        hand(ins, b, "dve")
                for which in (0, 2):
                    for j in range(6):
                        b = fill(ALL)
                        tt, ns, hs = score_bank(j)
                        q = slice(64 * (hs[0] % 2), 64 * (hs[0] % 2) + 64)
                        for i, h in enumerate(hs):
                            ins = mm(bank[b][:, i * ns:(i + 1) * ns], hT4[q, which, h // 2, tt * P:(tt + 1) * P],
                                     hT4[q, which + 1, h // 2, 0:ns], True, True)
                        hand(ins, b, "dve")
                    if which == 0:
                        gates(gates_after["dsa"])
                        def turn_probs(j):
                            eng.wait_ge(prob_act.sem, pe.at(prob_act, 12 * li + j + 1))
                            transposes(lambda i: pbuf[:, j, i * P:(i + 1) * P], 4, "act")
                            point("pT")

                        turn_probs(0)
                        for j in range(6):
                            tt, _, hs = score_bank(j)
                            if j < 5:
                                turn_probs(j + 1)
                            if j in (0, 2):
                                bo = fill(ALL)
                            eng.wait_ge(act_freed.sem, pe.point("pT", act_freed))
                            for i, h in enumerate(hs):
                                for s in range(tt + 1):
                                    c = (i * (tt + 1) + s) * P
                                    ins = mm(bank[bo][:, h * HD:(h + 1) * HD], pT[:, j % 2, c:c + P],
                                             kv[:, s, HALF + h * HD:HALF + (h + 1) * HD], s == 0, s == tt)
                            if j in (1, 5):
                                hand(ins, bo, "dve")
                        point("dsa")
                        eng.wait_ge(dve_freed.sem, pe.point("dsa", dve_freed))
                    else:
                        gates(gates_after["diff"])
                        for tt in range(TT):
                            bo = fill(ALL)
                            for jj in range(tt + 1):
                                eng.wait_ge(diff_dve.sem, pe.next(diff_dve))
                                transposes(lambda i: pbuf[:, 2 * (tt + jj), i * P:(i + 1) * P], 4, "act")
                                point("pT")
                                eng.wait_ge(act_freed.sem, pe.point("pT", act_freed))
                                for i in range(4):
                                    h = i if tt == 0 else 2 * jj + i // 2
                                    s = 0 if tt == 0 else i % 2
                                    ins = mm(bank[bo][:, h * P:(h + 1) * P], pT[:, (tt + jj) % 2, i * P:(i + 1) * P],
                                             zc(s, C_DV + h * P, P), s == 0, s == tt)
                            hand(ins, bo, "dve")
                        eng.wait_ge(yb_dve.sem, pe.next(yb_dve))
                    for half in range(2):
                        transposes(lambda i: yb[:, i % 2, (2 * half + i // 2) * P:(2 * half + i // 2 + 1) * P], 4,
                                   "act")
                point("branches")
                gates(len(g_left[0]))
                eng.wait_ge(act_freed.sem, pe.point("branches", act_freed))
                for br in range(3):
                    views = [take((2, 1024)), take((2, 1024))]
                    for tt in range(TT):
                        for h in range(2):
                            b = fill(ALL)
                            for k in range(4):
                                ins = mm(bank[b][:, :], yT[:, br, k, tt * P:(tt + 1) * P],
                                         views[k // 2][:, k % 2, h * HALF:(h + 1) * HALF], k == 0, k == 3)
                            hand(ins, b, "dve")
                    read_by(for_dve, 2)
                eng.wait_ge(mrg_dve.sem, pe.next(mrg_dve))
                for kp in range(4):
                    transposes(lambda i: xs[:, i % 2, (2 * kp + i // 2) * P:(2 * kp + i // 2 + 1) * P], 4,
                               "act" if kp % 2 == 0 else "dve")
                xnT_wait()
                to_x(xn_tile, KT, 4)
                ffn_input()
                ffn(groups1)

            def mlstm():
                eng.wait_ge(row_dve.sem, pe.next(row_dve))
                b = fill(ALL)
                for tt in range(TT):
                    ins = nc.tensor.transpose(bank[b][:, tt * 4:tt * 4 + 4], rowf[:, 5, tt * P:(tt + 1) * P],
                                              ident[0:4, 0:4])
                hand(ins, b, "dve")
                point("floor")
                eng.wait_ge(silu_act.sem, pe.next(silu_act, 8))
                eng.wait_ge(act_freed.sem, pe.point("z", act_freed))
                for h in range(4):
                    sel = ident[0:4, h:h + 1]
                    b = fill(ALL)
                    for o, s, t0, n in ((0, 0, 0, SEQ), (SEQ, 1, P, P)):
                        mm(bank[b][:, o:o + n], rowf[:, 2, s * P:(s + 1) * P], sel.broadcast_to([4, n]), True, False)
                        ins = mm(bank[b][:, o:o + n], sel.broadcast_to([4, P]), rowf[:, 4, t0:t0 + n], False, True)
                    hand(ins, b, "dve")
                    point("exponents")
                    b = fill(ALL)
                    for o, s, t0, n in ((0, 0, 0, SEQ), (SEQ, 1, P, P)):
                        ins = mm(bank[b][:, o:o + n], mqkT[:, 4 + h, s * P:(s + 1) * P], mqkT[:, h, t0:t0 + n],
                                 True, True)
                    hand(ins, b, "dve")
                    point("weights")
                for h in range(4):
                    eng.wait_ge(dve_freed.sem, pe.point("weights", dve_freed))
                    b = fill(ALL)
                    mm(bank[b][:, 0:129], pbuf[:, h, 0:P], v_ext[:, 0, h, :], True, True)
                    mm(bank[b][:, 129:258], pbuf[:, h, P:SEQ], v_ext[:, 0, h, :], True, False)
                    ins = mm(bank[b][:, 129:258], pbuf[:, h, SEQ:384], v_ext[:, 1, h, :], False, True)
                    hand(ins, b, "dve")
                eng.wait_ge(yb_dve.sem, pe.next(yb_dve))
                for half in range(2):
                    transposes(lambda i: yb[:, i % 2, (2 * half + i // 2) * P:(2 * half + i // 2 + 1) * P], 4, "act")

            for li in range(DEPTH):
                layer(li)

            norm_transposes()
            xnT_wait()
            for _ in range(4):
                feature_major("dve")
            for _ in range(8):
                chunk(512, "act")
            point("ret_v")
            eng.wait_ge(ret_dve.sem, pe.next(ret_dve, 8))
            for h in range(RH):
                b = fill(ALL)
                for o, s, t0, n in ((0, 0, 0, SEQ), (SEQ, 1, P, P)):
                    for k in range(2):
                        ins = mm(bank[b][:, o:o + n], qT2[:, 8 + 2 * h + k, s * P:(s + 1) * P],
                                 qT2[:, 2 * h + k, t0:t0 + n], k == 0, k == 1)
                hand(ins, b, "dve")
                point("ret_w")
            eng.wait_ge(act_freed.sem, pe.point("ret_v", act_freed))
            for h in range(RH):
                eng.wait_ge(dve_freed.sem, pe.point("ret_w", dve_freed))
                b = fill(ALL)
                ins = mm(bank[b][:, :], pbuf[:, h, 0:P], rv[:, 0, h * HALF:(h + 1) * HALF], True, True)
                hand(ins, b, "act")
                b = fill(ALL)
                mm(bank[b][:, :], pbuf[:, h, P:SEQ], rv[:, 0, h * HALF:(h + 1) * HALF], True, False)
                ins = mm(bank[b][:, :], pbuf[:, h, SEQ:384], rv[:, 1, h * HALF:(h + 1) * HALF], False, True)
                hand(ins, b, "act")
            point("ret_o")
            eng.wait_ge(rets_dve.sem, pe.next(rets_dve))
            for fp in range(8):
                transposes(lambda i: rv[:, i % 2, (2 * fp + i // 2) * P:(2 * fp + i // 2 + 1) * P], 4, "act")
            point("ret_oT")
            eng.wait_ge(act_freed.sem, pe.point("ret_oT", act_freed))
            to_x(lambda k, tt: oT2[:, k, tt * P:(tt + 1) * P], 16, 8)
            ffn_input()
            ffn(groups2)

            norm_transposes()
            xnT_wait()
            for part, who in (("C", "act"), ("h", "dve"), ("B", "act")):
                for _ in range(2):
                    feature_major(who)
                point("conv2 " + part)
            eng.wait_ge(conv2_dve.sem, pe.next(conv2_dve))
            to_x(lambda k, tt: cyT[:, k, tt * P:(tt + 1) * P], KT, 4)

            norm_transposes()
            xnT_wait()
            b = fill(ALL)
            for tt in range(TT):
                for k in range(KT):
                    ins = mm(bank[b][:, tt * NE:(tt + 1) * NE], xn_tile(k, tt), w_rt[:, k, :], k == 0, k == KT - 1)
            hand(ins, b, "dve")
            eng.wait_ge(mask_dve.sem, pe.next(mask_dve))
            b = fill(ALL)
            m = [rt[:, R_MASK, tt, :] for tt in range(TT)]
            ut = const[:, K_UT:K_UT + P]
            mm(bank[b][:, 0:8], ut, m[0], True, True)
            mm(bank[b][:, 8:16], ones, m[0], True, False)
            mm(bank[b][:, 8:16], ut, m[1], False, True)
            mm(bank[b][:, 16:24], ones, m[0], True, False)
            ins = mm(bank[b][:, 16:24], ones, m[1], False, True)
            hand(ins, b, "dve")
            point("slots")
            eng.wait_ge(dve_freed.sem, pe.point("slots", dve_freed))

            def gather(big):
                eng.wait_ge(pick_dve.sem, pe.next(pick_dve))
                for kp in range(4):
                    b = fill(LOW)

                    def half(s):
                        for j in range(2):
                            for tt in range(TT):
                                k = 2 * kp + j
                                ins = mm(bank[b][:, j * SEQ + s * P:j * SEQ + (s + 1) * P],
                                         xs[:, tt, k * P:(k + 1) * P], pick[:, tt, s * P:(s + 1) * P],
                                         tt == 0, tt == 1)
                        return ins
                    with eng.If(big):
                        half(1)
                    hand(half(0), b, "act")
                    point("input")
                    give_low(b)

            def tokens(e):
                return eng.value_load(cnt[0:1, bass.ds(e, 1)], min_val=0, max_val=SEQ)

            gather(tokens(0) > P)
            before = (for_act.marked, for_dve.marked)
            with pe.trips(NE, signals) as e:
                eng.wait_ge(act_freed.sem, pe.at(act_freed, before[0]))
                eng.wait_ge(dve_freed.sem, pe.at(dve_freed, before[1]))
                eng.wait_ge(x_low.sem, pe.at(x_low, x_low.marked))
                last.clear()
                big, big_next = tokens(e) > P, tokens(e + 1) > P
                b = fill((4, 5))
                for s in range(2):
                    for tt in range(TT):
                        ins = nc.tensor.transpose(bank[b][:, s * SEQ + tt * P:s * SEQ + (tt + 1) * P],
                                                  pickg[:, tt, s * P:(s + 1) * P], ident)
                hand(ins, b, "dve")
                ffn(groups2, big, lambda: gather(big_next))
                eng.wait_ge(act_freed.sem, pe.point("y", act_freed))
                eng.wait_ge(dve_freed.sem, pe.point("y", dve_freed))
                for tt in range(TT):
                    for h in range(2):
                        b = fill(LOW)
                        o = bank[b][:, :]
                        l = [putT[:, s, tt * P:(tt + 1) * P] for s in range(2)]
                        r = [ysb[:, s, h * HALF:(h + 1) * HALF] for s in range(2)]
                        with eng.If(big):
                            mm(o, l[1], r[1], True, False)
                            two = mm(o, l[0], r[0], False, True)
                            two.then_inc(for_dve.sem, 1)
                        with eng.Else():
                            one = mm(o, l[0], r[0], True, True)
                            hand(one, b, "dve")
            issued[0] += (NE - 1) * EXPERT_UNITS
            n_split[0] += (NE - 1) * EXPERT_SPLIT
            point("x")

        @block.scalar
        def _(eng):
            act = Engine(eng, "act", points)
            nth = [0]
            points_x = [False]

            def A(out, in_, func, **kw):
                return nc.scalar.activation(out, in_, func, **kw)

            def take():
                eng.wait_ge(for_act.sem, act.next(for_act))
                nth[0] += 1
                return bank[act_banks[nth[0] - 1]]

            def copy(dst, n=HALF, view=None, scale=1.0):
                b = take()
                ins = A(dst, b[:, 0:n] if view is None else view(b), ACT.Copy, scale=scale)
                return ins.then_inc(act_freed.sem, act_freed.tick())

            def roots(o, i):
                eng.wait_ge(mean_sq.sem, act.next(mean_sq))
                A(o, i, ACT.Sqrt).then_inc(root.sem, root.tick())

            def evac_features(gain, dst, pairs):
                for kp in pairs:
                    b = take()
                    for j in range(2):
                        k = 2 * kp + j
                        g = 1.0 if gain is None else gcol[:, gain + k:gain + k + 1]
                        ins = A(dst[:, k, :], b[:, j * SEQ:(j + 1) * SEQ], ACT.Copy, scale=g)
                    ins.then_inc(act_freed.sem, act_freed.tick())

            def norm_root():
                if points_x[0]:
                    eng.wait_ge(dve_freed.sem, act.point("x", dve_freed))
                points_x[0] = True
                for tt in range(TT):
                    ins = A(xs[:, tt, :], x[:, tt, :], ACT.Square, accum_out=xsum[:, 0, tt:tt + 1])
                ins.then_inc(squares.sem, squares.tick())
                roots(xsum[:, 2, :], xsum[:, 1, :])

            def highs(gain):
                for kp in range(4):
                    b = take()
                    for j in range(2):
                        k = 2 * kp + j
                        ins = A(parts[:, 0, k, :], b[:, j * SEQ:(j + 1) * SEQ], ACT.Copy,
                                scale=gcol[:, gain + k:gain + k + 1])
                    ins.then_inc(act_freed.sem, act_freed.tick())

            def norm(gain, evacuate=None):
                norm_root()
                eng.wait_ge(rstd_dve.sem, act.next(rstd_dve))
                A(xs[:, 1, :], x[:, 1, :], ACT.Copy, scale=xsum[:, 3, 1:2]).then_inc(xs_act.sem, xs_act.tick())
                if evacuate is None:
                    evac_features(gain, xnT, (0, 2))
                else:
                    evacuate(gain)

            nth_split = [len(unit_of_split) - EXPERT_SPLIT]

            def expert_high(units):
                for _ in range(units):
                    n, m = unit_of_split[nth_split[0]], nth_split[0]
                    nth_split[0] += 1
                    arrived = loaded[n % RING]
                    eng.wait_ge(arrived.sem, act.at(arrived, 16 * (n // RING + 1)))
                    sig, value = split_read[m - SPLITS]
                    if m - SPLITS < len(unit_of_split) - EXPERT_SPLIT:
                        sig, value = split_read[m - SPLITS + EXPERT_SPLIT]
                        value -= sig.per_trip
                    eng.wait_ge(sig.sem, act.at(sig, value))
                    A(split[:, m % SPLITS, 0, :], ring[:, n % RING, :], ACT.Copy).then_inc(high_act.sem, high_act.tick())

            def ffn_act(groups, dense):
                for i in range(len(groups) + 1):
                    if not dense and i < len(groups):
                        expert_high(2 * group_units(i, groups)[0])
                    if i:
                        n = groups[i - 1][1]
                        if not dense:
                            copy(hT[:, 0, :, :].rearrange("p f t -> p (f t)")[:, 0:n], n)
                        for tt in (1, 0) if dense else ():
                            copy(parts[:, 0, KT:KT + n // P, tt * P:(tt + 1) * P],
                                 view=lambda b: b[:, 0:n].rearrange("p (f t) -> p f t", t=P))
                    if i < len(groups):
                        n = groups[i][1]
                        for tt in (1, 0):
                            b = take()
                            ins = A(sg[:, tt, 0:n], b[:, 0:n], ACT.Silu)
                            ins.then_inc(act_freed.sem, act_freed.tick())

            def layer(li):
                norm(G_MIX + 8 * li)
                for c in range(4):
                    copy(cpad[:, 2 * c:2 * c + 2, 3:SEQ + 3], view=lambda b: b[:, :].rearrange("p (f t) -> p f t", f=2))

                def z_evac(col, n):
                    for tt in range(TT):
                        if col == C_V:
                            copy(v_ext[:, tt, :, 0:M_DH], view=lambda b: b[:, :].rearrange("p (h d) -> p h d", h=4))
                        else:
                            copy(zc(tt, col, n), n)

                left = list(g_chunks)

                def gates(m):
                    for _ in range(m):
                        z_evac(*left.pop(0))

                z_evac(*z_chunks[0])
                eng.wait_ge(absf_dve.sem, act.next(absf_dve))
                A(rowf[:, 6, :], rowf[:, 6, :], ACT.Exp, scale=-1.0).then_inc(act_step.sem, act_step.tick())
                eng.wait_ge(act_step.sem, act.latest(act_step))
                A(rowf[:, 6, :], rowf[:, 6, :], ACT.Ln, bias=1.0).then_inc(logf_act.sem, logf_act.tick())
                z_evac(*z_chunks[1])
                z_evac(*z_chunks[2])
                z_evac(*z_chunks[3])
                for f in range(KT):
                    eng.wait_ge(conv_dve.sem, act.next(conv_dve))
                    A(mqkT[:, f, :], mqkT[:, f, :], ACT.Silu).then_inc(silu_act.sem, silu_act.tick())
                for c in z_chunks[4:]:
                    z_evac(*c)
                roots(hsum[:, 2, kA:kB], hsum[:, 1, kA:kB])
                gates(gates_after["z"])
                for tt in range(TT):
                    for h in range(2):
                        copy(kv[:, tt, h * HALF:(h + 1) * HALF])
                roots(hsum[:, 2, kB:kY], hsum[:, 1, kB:kY])
                gates(gates_after["kv"])
                eng.wait_ge(dve_freed.sem, act.point("floor", dve_freed))
                A(floor[:, 1, :], floor[:, 0, :], ACT.Exp).then_inc(floor_act.sem, floor_act.tick())
                for h in range(M_HEADS):
                    eng.wait_ge(dve_freed.sem, act.point("exponents", dve_freed))
                    A(pbuf[:, h, 0:384], pbuf[:, h, 0:384], ACT.Exp).then_inc(decay_act.sem, decay_act.tick())
                roots(hsum[:, 2, kY:kY + 8], hsum[:, 1, kY:kY + 8])
                for tt in range(TT):
                    A(zc(tt, C_O, HALF), zc(tt, C_O, HALF), ACT.Sigmoid).then_inc(sig_act.sem, sig_act.tick())
                evac_features(G_MN + 4 * li, yT[:, 0, :, :], (0, 1))
                gates(gates_after["mlstm"])
                for w in range(4):
                    for half in range(2):
                        copy(hT4[:, w, 2 * half:2 * half + 2, :].rearrange("p f t -> p (f t)"))
                copy(iqT[:, :, :].rearrange("p f t -> p (f t)"))
                copy(ikT[:, :], SEQ)

                def exps():
                    for j in range(6):
                        tt, ns, hs = score_bank(j)
                        eng.wait_ge(score_dve.sem, act.next(score_dve))
                        for i, h in enumerate(hs):
                            h += 8 * tt
                            s = pbuf[:, j, i * ns:(i + 1) * ns]
                            ins = A(s, s, ACT.Exp, bias=nmax[:, h:h + 1], accum_out=psum_row[:, 0, h:h + 1])
                        ins.then_inc(prob_act.sem, prob_act.tick())

                exps()
                gates(gates_after["dsa"])
                for j in range(6):
                    copy(pT[:, j % 2, :])
                evac_features(None, yT[:, 1, :, :], (0, 1))
                exps()
                gates(gates_after["diff"])
                for j in range(3):
                    copy(pT[:, j % 2, :])
                roots(hsum[:, 2, kY:kY + 8], hsum[:, 1, kY:kY + 8])
                for half in range(2):
                    b = take()
                    ins = A(yT[:, 2, 2 * half:2 * half + 2, :].rearrange("p f t -> p (f t)"), b[:, :], ACT.Copy,
                            scale=dgain[:, li:li + 1])
                    ins.then_inc(act_freed.sem, act_freed.tick())
                gates(len(left))
                eng.wait_ge(act_freed.sem, act.latest(act_freed))
                for tt in range(TT):
                    A(zc(tt, C_G, 3 * D), zc(tt, C_G, 3 * D), ACT.Sigmoid).then_inc(sig_act.sem, sig_act.tick())
                evac_features(None, xnT, (0, 2))
                norm(G_FFN + 8 * li, highs)
                ffn_act(groups1, True)

            eng.wait_ge(params.sem, act.next(params, 16 * PARAMS))
            eng.wait_ge(setup_dve.sem, act.next(setup_dve))
            eng.wait_ge(lam_dve.sem, act.next(lam_dve))
            A(lam[:, 1, :], lam[:, 0, :], ACT.Exp).then_inc(lam_act.sem, lam_act.tick())
            for li in range(DEPTH):
                layer(li)

            norm(G_MIX0)
            for c in range(8):
                dst = rv if c < 4 else rg
                for tt in range(TT):
                    copy(dst[:, tt, (c % 4) * HALF:(c % 4 + 1) * HALF])
            eng.wait_ge(act_freed.sem, act.latest(act_freed))
            for tt in range(TT):
                ins = A(rg[:, tt, :], rg[:, tt, :], ACT.Silu)
            ins.then_inc(rsilu_act.sem, rsilu_act.tick())
            for h in range(RH):
                bs = [take(), take()]
                for tt in range(TT):
                    A(rv[:, tt, h * HALF:(h + 1) * HALF], bs[tt][:, :], ACT.Copy)
                    ins = A(tmp[:, tt, :], bs[tt][:, :], ACT.Square, accum_out=hsum[:, 0, tt * 4 + h:tt * 4 + h + 1])
                    ins.then_inc(act_freed.sem, act_freed.tick())
                eng.wait_ge(act_freed.sem, act.latest(act_freed))
            roots(hsum[:, 2, 0:8], hsum[:, 1, 0:8])
            evac_features(None, oT2, range(8))
            norm(G_FFN0, highs)
            ffn_act(groups2, True)

            norm(G_MIX1)
            for dst in (cC, cB):
                for c in range(4):
                    copy(dst[:, 2 * c:2 * c + 2, :].rearrange("p f t -> p (f t)"))

            norm(G_FFN1)
            eng.wait_ge(diff2_dve.sem, act.next(diff2_dve))
            A(rt2[:, 3, :], rt2[:, 2, :], ACT.Exp).then_inc(exp2_act.sem, exp2_act.tick())
            highs(G_FFN1)
            with act.trips(NE, signals):
                ffn_act(groups2, False)
                highs(G_FFN1)
                for h in range(2):
                    copy(ysb[:, 0, h * HALF:(h + 1) * HALF])
            norm_root()

        @block.vector
        def _(eng):
            dve = Engine(eng, "dve", points)
            V = nc.vector
            nth, nth_low, nth_split = [0], [0], [0]
            dense_splits = len(unit_of_split) - EXPERT_SPLIT

            def take():
                eng.wait_ge(for_dve.sem, dve.next(for_dve))
                nth[0] += 1
                return bank[dve_banks[nth[0] - 1]]

            def then(ins):
                ins.then_inc(dve_step.sem, dve_step.tick())
                eng.wait_ge(dve_step.sem, dve.latest(dve_step))

            def emptied(ins):
                ins.then_inc(dve_freed.sem, dve_freed.tick())
                eng.wait_ge(dve_freed.sem, dve.latest(dve_freed))

            def bc(ap, n):
                return ap.unsqueeze(len(ap.shape)).broadcast_to([*ap.shape, n])

            def mean_squares(o, i, n):
                V.tensor_scalar(o, i, 1.0 / n, EPS, ALU.mult, ALU.add).then_inc(mean_sq.sem, mean_sq.tick())

            def inverse_root(tile, cols):
                eng.wait_ge(root.sem, dve.next(root))
                return V.reciprocal(tile[:, 3, cols], tile[:, 2, cols])

            def norm_inverse():
                eng.wait_ge(squares.sem, dve.next(squares))
                mean_squares(xsum[:, 1, :], xsum[:, 0, :], D)
                ins = inverse_root(xsum, slice(0, TT))
                ins.then_inc(rstd_dve.sem, rstd_dve.tick())
                eng.wait_ge(rstd_dve.sem, dve.latest(rstd_dve))

            def evac_features(gain):
                for kp in (1, 3):
                    b = take()
                    for j in range(2):
                        k = 2 * kp + j
                        o, i = xnT[:, k, :], b[:, j * SEQ:(j + 1) * SEQ]
                        if gain is None:
                            ins = V.tensor_copy(o, i)
                        else:
                            ins = V.tensor_scalar(o, i, gcol[:, gain + k:gain + k + 1], None, ALU.mult)
                    ins.then_inc(dve_freed.sem, dve_freed.tick())

            def norm(gain, evacuate=None):
                norm_inverse()
                V.tensor_scalar(xs[:, 0, :], x[:, 0, :], xsum[:, 3, 0:1], None,
                                ALU.mult).then_inc(xs_dve.sem, xs_dve.tick())
                (evacuate or evac_features)(gain)

            def first_lows(gain):
                weights_low(1)
                lows(gain)

            def lows(gain):
                for kp in range(4):
                    eng.wait_ge(act_freed.sem, dve.point("input", act_freed))
                    b = bank[low_banks[nth_low[0]]]
                    nth_low[0] += 1
                    for j in range(2):
                        k = 2 * kp + j
                        ins = V.scalar_tensor_tensor(parts[:, 1, k, :], b[:, j * SEQ:(j + 1) * SEQ],
                                                     gcol[:, gain + k:gain + k + 1], parts[:, 0, k, :].bitcast(F32),
                                                     ALU.mult, ALU.subtract)
                    ins.then_inc(x_low.sem, 1)

            def weights_low(units):
                for _ in range(units):
                    n, m = unit_of_split[nth_split[0]], nth_split[0]
                    nth_split[0] += 1
                    if m < dense_splits:
                        eng.wait_ge(high_made.sem, dve.at(high_made, m + 1))
                    else:
                        eng.wait_ge(high_act.sem, dve.at(high_act, m - dense_splits + 1))
                    V.tensor_tensor(split[:, m % SPLITS, 1, :], ring[:, n % RING, :],
                                    split[:, m % SPLITS, 0, :].bitcast(F32),
                                    ALU.subtract).then_inc(low_made.sem, low_made.tick())

            def add_to_x(tiles=(0, 1)):
                for tt in tiles:
                    for h in range(2):
                        b = take()
                        o = x[:, tt, h * HALF:(h + 1) * HALF]
                        ins = V.tensor_tensor(o, b[:, :], o, ALU.add)
                        ins.then_inc(dve_freed.sem, dve_freed.tick())
                eng.wait_ge(dve_freed.sem, dve.latest(dve_freed))

            def ffn_dve(groups, dense, next_picks=None):
                for i in range(len(groups) + 1):
                    up, dn = group_units(i, groups)
                    if dense:
                        weights_low((up or dn) - (1 if i < 2 else 0))
                    elif up:
                        weights_low(up + (1 if i < 2 else 0))
                    if i and not dense:
                        n = groups[i - 1][1]
                        b = take()
                        V.tensor_copy(hT[:, 1, :, :].rearrange("p f t -> p (f t)")[:, 0:n],
                                      b[:, 0:n]).then_inc(dve_freed.sem, dve_freed.tick())
                    if i and dense:
                        n = groups[i - 1][1]
                        eng.wait_ge(act_freed.sem, dve.point("turned", act_freed))
                        for tt in (1, 0):
                            b = bank[low_banks[nth_low[0]]]
                            nth_low[0] += 1
                            f = slice(KT, KT + n // P)
                            c = slice(tt * P, (tt + 1) * P)
                            V.tensor_tensor(parts[:, 1, f, c], b[:, 0:n].rearrange("p (f t) -> p f t", t=P),
                                            parts[:, 0, f, c].bitcast(F32),
                                            ALU.subtract).then_inc(hidden_low.sem, 1)
                    if dense and up:
                        weights_low(up + dn)
                    if i == 0:
                        weights_low(1)
                    elif not dense and i + 1 < len(groups):
                        weights_low(group_units(i + 1, groups)[0])
                    if i < len(groups):
                        n = groups[i][1]
                        eng.wait_ge(act_freed.sem, dve.point("gate", act_freed))
                        for tt in (1, 0):
                            b = take()
                            ins = V.tensor_tensor(hb[:, tt, 0:n], b[:, 0:n], sg[:, tt, 0:n], ALU.mult)
                            ins.then_inc(dve_freed.sem, dve_freed.tick())
                    if not dense and i == 2:
                        next_picks()

            def heads_sum(src, n_heads, width, o):
                sq = tmp[:, 0, 0:n_heads * width].rearrange("p (h d) -> p h d", h=n_heads)
                then(V.tensor_tensor(sq, src, src, ALU.mult))
                then(V.tensor_reduce(o, sq, AX.X, ALU.add))

            def heads(ap, h):
                return ap.rearrange("p (h d) -> p h d", h=h)

            def rope(src, nh, tt, inverse, gain, dst=None, done=None):
                a = heads(tmp[:, 0, 0:nh * HD], nh)
                t = heads(tmp[:, 1, 0:nh * HD], nh)
                v = heads(src, nh)
                if inverse is not None:
                    then(V.tensor_tensor(a, v, bc(inverse, HD), ALU.mult))
                    then(V.tensor_tensor(a, a, gain.unsqueeze(1).broadcast_to([P, nh, HD]), ALU.mult))
                    v = a
                c2 = const[:, K_C2 + tt * HD:K_C2 + (tt + 1) * HD].unsqueeze(1).broadcast_to([P, nh, HD])
                s2 = const[:, K_S2 + tt * HD:K_S2 + (tt + 1) * HD].unsqueeze(1).broadcast_to([P, nh, HD])
                H = HD // 2
                V.tensor_tensor(t[:, :, 0:H], v[:, :, H:HD], s2[:, :, 0:H], ALU.mult)
                then(V.tensor_tensor(t[:, :, H:HD], v[:, :, 0:H], s2[:, :, H:HD], ALU.mult))
                then(V.tensor_tensor(a, v, c2, ALU.mult))
                ins = V.tensor_tensor(heads(src, nh) if dst is None else dst, a, t, ALU.add)
                sig = done or dve_step
                ins.then_inc(sig.sem, sig.tick())
                eng.wait_ge(sig.sem, dve.latest(sig))

            eng.wait_ge(params.sem, dve.next(params, 16 * PARAMS))
            b = take()
            emptied(V.tensor_copy(gcol[:, :], b[:, 0:G_ROWS]))
            for li in range(DEPTH):
                lam_init = 0.8 - 0.6 * math.exp(-0.3 * li)
                ins = V.tensor_scalar(dgain[:, li:li + 1], gcol[:, G_DO + li:G_DO + li + 1], 1.0 - lam_init, None,
                                      ALU.mult)
            ins.then_inc(setup_dve.sem, setup_dve.tick())
            eng.wait_ge(setup_dve.sem, dve.latest(setup_dve))
            pairs = lamv[:, :, :, :].rearrange("p l (a b) d -> p (l a) b d", b=2)
            prod = tmp[:, 0, 0:2 * DEPTH * HD].rearrange("p (n d) -> p n d", d=HD)
            then(V.tensor_tensor(prod, pairs[:, :, 0, :], pairs[:, :, 1, :], ALU.mult))
            V.tensor_reduce(lam[:, 0, :], prod, AX.X, ALU.add).then_inc(lam_dve.sem, lam_dve.tick())
            eng.wait_ge(lam_dve.sem, dve.latest(lam_dve))
            eng.wait_ge(lam_act.sem, dve.next(lam_act))
            for li in range(DEPTH):
                lam_init = 0.8 - 0.6 * math.exp(-0.3 * li)
                then(V.tensor_tensor(lam[:, 2, li:li + 1], lam[:, 1, 2 * li + 1:2 * li + 2], lam[:, 1, 2 * li:2 * li + 1],
                                     ALU.subtract))
                then(V.tensor_scalar(lam[:, 3, li:li + 1], lam[:, 2, li:li + 1], lam_init, None, ALU.subtract))

            def mlstm_rows(li):
                b = take()
                V.memset(rowf[:, 7, :], 1.0)
                V.memset(cpad[:, :, 0:3], 0.0)
                V.memset(v_ext[:, :, :, M_DH:M_DH + 1], 1.0)
                for g in range(2):
                    ins = V.tensor_scalar(rowf[:, g, :], b[0:4, g * SEQ:(g + 1) * SEQ],
                                          gateb[:, 2 * li + g:2 * li + g + 1], None, ALU.add)
                emptied(ins)
                f, i, B, cm = rowf[:, 1, :], rowf[:, 0, :], rowf[:, 3, :], rowf[:, 4, :]
                V.scalar_tensor_tensor(rowf[:, 6, :], f, -1.0, f, ALU.mult, ALU.max).then_inc(absf_dve.sem, absf_dve.tick())
                return f, i, B, cm

            def mlstm_scans(f, i, B, cm):
                eng.wait_ge(logf_act.sem, dve.next(logf_act))
                then(V.scalar_tensor_tensor(f, f, 0.0, rowf[:, 6, :], ALU.min, ALU.subtract))
                then(V.tensor_tensor_scan(B, rowf[:, 7, :], f, 0.0, ALU.mult, ALU.add))
                then(V.tensor_tensor(rowf[:, 2, :], i, B, ALU.subtract))
                then(V.tensor_tensor_scan(cm, rowf[:, 7, :], rowf[:, 2, :], NEG, ALU.mult, ALU.max))
                then(V.scalar_tensor_tensor(rowf[:, 5, :], B, -1.0, cm, ALU.mult, ALU.subtract))
                V.tensor_scalar(cm, cm, -1.0, None, ALU.mult).then_inc(row_dve.sem, row_dve.tick())
                eng.wait_ge(row_dve.sem, dve.latest(row_dve))

            def convolve(li):
                for f in range(KT):
                    if f % 4 == 0:
                        eng.wait_ge(act_freed.sem, dve.point("qk", act_freed))
                    w = [gcol[:, G_CW + (li * 4 + j) * KT + f:G_CW + (li * 4 + j) * KT + f + 1] for j in range(4)]
                    o = mqkT[:, f, :]
                    then(V.tensor_scalar(o, cpad[:, f, 0:SEQ], w[0], gcol[:, G_CB + li * KT + f:G_CB + li * KT + f + 1],
                                         ALU.mult, ALU.add))
                    for j in range(1, 4):
                        ins = V.scalar_tensor_tensor(o, cpad[:, f, j:j + SEQ], w[j], o, ALU.mult, ALU.add)
                        if j < 3:
                            then(ins)
                    ins.then_inc(conv_dve.sem, conv_dve.tick())

            def out_norm():
                for tt in range(TT):
                    heads_sum(heads(yb[:, tt, :], 4), 4, P, hsum[:, 0, kY + 4 * tt:kY + 4 * tt + 4])
                mean_squares(hsum[:, 1, kY:kY + 8], hsum[:, 0, kY:kY + 8], P)
                then(inverse_root(hsum, slice(kY, kY + 8)))
                for tt in range(TT):
                    y = heads(yb[:, tt, :], 4)
                    ins = V.tensor_tensor(y, y, bc(hsum[:, 3, kY + 4 * tt:kY + 4 * tt + 4], P), ALU.mult)
                return ins

            def mlstm():
                b = take()
                V.tensor_copy(floor[:, 0, :], b[:, 0:8]).then_inc(dve_freed.sem, dve_freed.tick())
                for h in range(M_HEADS):
                    b = take()
                    ins = V.tensor_tensor(pbuf[:, h, 0:384], b[:, 0:384], const[:, K_CMT:K_CMT + 384], ALU.add)
                    ins.then_inc(dve_freed.sem, dve_freed.tick())
                    b = take()
                    eng.wait_ge(decay_act.sem, dve.next(decay_act))
                    ins = V.scalar_tensor_tensor(pbuf[:, h, 0:384], b[:, 0:384], M_DH ** -0.5, pbuf[:, h, 0:384],
                                                 ALU.mult, ALU.mult)
                    ins.then_inc(dve_freed.sem, dve_freed.tick())
                eng.wait_ge(floor_act.sem, dve.next(floor_act))
                for h in range(M_HEADS):
                    b = take()
                    nd = b[:, 0:258].rearrange("p (t c) -> p t c", t=TT)
                    fl = floor[:, 1, :].rearrange("p (t h) -> p t h", t=TT)[:, :, h]
                    d = floor[:, 2, 2 * (h % 2):2 * (h % 2) + 2]
                    r = floor[:, 3, 2 * h:2 * h + 2]
                    then(V.tensor_scalar(d, nd[:, :, 128], -1.0, None, ALU.mult))
                    then(V.tensor_tensor(d, nd[:, :, 128], d, ALU.max))
                    then(V.tensor_tensor(d, d, fl, ALU.max))
                    then(V.reciprocal(r, d))
                    for tt in range(TT):
                        ins = V.tensor_scalar(yb[:, tt, h * P:(h + 1) * P], nd[:, tt, 0:128], r[:, tt:tt + 1], None,
                                              ALU.mult)
                    emptied(ins)
                then(out_norm())
                for tt in range(TT):
                    eng.wait_ge(sig_act.sem, dve.next(sig_act))
                    ins = V.tensor_tensor(yb[:, tt, :], yb[:, tt, :], zc(tt, C_O, HALF), ALU.mult)
                ins.then_inc(yb_dve.sem, yb_dve.tick())

            def top_keys():
                for tt in range(TT):
                    n, o = (P, 0) if tt == 0 else (SEQ, P)
                    acc = idx[:, o:o + n]
                    for n_th, h in enumerate((0, 2, 1, 3)):
                        if h < 2:
                            b = take()
                        ps = b[:, h // 2 * n:(h // 2 + 1) * n]
                        w = iw[:, tt, h:h + 1]
                        t = acc if h == 0 else tmp[:, n_th % 2, 0:n]
                        ins = V.tensor_scalar(t, ps, 0.0, w, ALU.max, ALU.mult)
                        if h > 1:
                            emptied(ins)
                        else:
                            then(ins)
                        if h:
                            then(V.tensor_tensor(acc, acc, t, ALU.add))
                    d = idx[:, o + n - P:o + n]
                    then(V.tensor_tensor(d, d, const[:, K_DIAG:K_DIAG + P], ALU.add))
                    wk = work[:, o:o + n]
                    for r in range(TOPK // 8):
                        src = acc if r == 0 else wk
                        then(V.max(top8[:, :], src))
                        then(V.match_replace(wk, top8[:, :], src, TAKEN))
                    m = msel[:, o:o + n]
                    then(V.tensor_tensor(m, wk, acc, ALU.not_equal))
                    then(V.tensor_scalar(m, m, 1.0, -NEG, ALU.subtract, ALU.mult))
                    d = msel[:, o + n - P:o + n]
                    then(V.tensor_tensor(d, d, const[:, K_DIAG:K_DIAG + P], ALU.add))

            def scores(mask):
                for j in range(6):
                    tt, ns, hs = score_bank(j)
                    nh = len(hs)
                    mx = nmax[:, 8 * tt + hs[0]:8 * tt + hs[-1] + 1:2]
                    s = heads(pbuf[:, j, :], nh)
                    b = take()
                    m = mask(tt).unsqueeze(1).broadcast_to([P, nh, ns])
                    emptied(V.scalar_tensor_tensor(s, heads(b[:, :], nh), HD ** -0.5, m, ALU.mult, ALU.add))
                    then(V.tensor_reduce(mx, s, AX.X, ALU.max))
                    V.tensor_scalar(mx, mx, -1.0, None, ALU.mult).then_inc(score_dve.sem, score_dve.tick())
                    eng.wait_ge(score_dve.sem, dve.latest(score_dve))

            def layer(li):
                norm(G_MIX + 8 * li)
                rows = mlstm_rows(li)
                convolve(li)
                mlstm_scans(*rows)
                eng.wait_ge(act_freed.sem, dve.point("z", act_freed))
                for tt in range(TT):
                    o = kA + 25 * tt
                    for i, (col, nh, w) in enumerate(((C_SQ, 8, HD), (C_DQ, 8, HD), (C_DK, 8, HD), (C_CKV, 1, 256))):
                        heads_sum(heads(zc(tt, col, nh * w), nh), nh, w, hsum[:, 0, o + 8 * i:o + 8 * i + nh])
                s, m = (hsum[:, i, kA:kB].rearrange("p (t c) -> p t c", t=TT) for i in range(2))
                V.tensor_scalar(m[:, :, 24:25], s[:, :, 24:25], 1.0 / KV_RANK, EPS, ALU.mult, ALU.add)
                mean_squares(m[:, :, 0:24], s[:, :, 0:24], HD)
                then(inverse_root(hsum, slice(kA, kB)))
                for tt in range(TT):
                    ins = V.tensor_scalar(yb[:, tt, 0:256], zc(tt, C_CKV, 256), hsum[:, 3, kA + 25 * tt + 24:kA + 25 * tt + 25],
                                          None, ALU.mult)
                ins.then_inc(kvn_dve.sem, kvn_dve.tick())

                def rope_from_z(cols):
                    for tt in range(TT):
                        for col, i in cols:
                            c = kA + 25 * tt + 8 * i
                            rope(zc(tt, col, 512), 8, tt, hsum[:, 3, c:c + 8], qk_gain[:, (0, 2, 3)[i], li, :])

                rope_from_z(((C_SQ, 0),))
                b = take()
                for k in range(2):
                    g = G_KV + 2 * li + k
                    ins = V.tensor_scalar(ckvT[:, k, :], b[:, k * SEQ:(k + 1) * SEQ], gcol[:, g:g + 1], None, ALU.mult)
                ins.then_inc(dve_freed.sem, dve_freed.tick())
                rope_from_z(((C_DQ, 1), (C_DK, 2)))
                for tt in range(TT):
                    rope(zc(tt, C_IQ, 256), 4, tt, None, None)
                    both = tmp[:, 3, tt * P:(tt + 1) * P]
                    rope(zc(tt, C_IK, HD), 1, tt, None, None, dst=heads(both[:, 0:HD], 1))
                    then(V.tensor_copy(both[:, HD:P], both[:, 0:HD]))
                    then(V.tensor_scalar(iw[:, tt, :], zc(tt, C_IW, IDX_HEADS), (IDX_HEADS * HD) ** -0.5, None, ALU.mult))
                eng.wait_ge(act_freed.sem, dve.point("kv", act_freed))
                for tt in range(TT):
                    heads_sum(heads(kv[:, tt, 0:HALF], 8), 8, HD, hsum[:, 0, kB + 8 * tt:kB + 8 * tt + 8])
                mean_squares(hsum[:, 1, kB:kY], hsum[:, 0, kB:kY], HD)
                then(inverse_root(hsum, slice(kB, kY)))
                for tt in range(TT):
                    rope(kv[:, tt, 0:HALF], 8, tt, hsum[:, 3, kB + 8 * tt:kB + 8 * tt + 8], qk_gain[:, 1, li, :],
                         done=rope_dve if tt else None)
                mlstm()
                top_keys()

                scores(lambda tt: msel[:, 0:P] if tt == 0 else msel[:, P:384])
                eng.wait_ge(prob_act.sem, dve.at(prob_act, 12 * li + 6))
                then(V.reciprocal(psum_row[:, 1, :], psum_row[:, 0, :]))
                for tt in range(TT):
                    b = take()
                    ins = V.tensor_tensor(heads(yb[:, tt, :], 8), heads(b[:, :], 8), bc(psum_row[:, 1, 8 * tt:8 * tt + 8], HD),
                                          ALU.mult)
                    ins.then_inc(dve_freed.sem, dve_freed.tick())

                scores(lambda tt: const[:, K_DIAG:K_DIAG + P] if tt == 0 else causal2)
                eng.wait_ge(prob_act.sem, dve.at(prob_act, 12 * li + 12))
                then(V.reciprocal(psum_row[:, 1, :], psum_row[:, 0, :]))
                then(V.tensor_scalar(psum_row[:, 2, :], psum_row[:, 1, :], lam[:, 3, li:li + 1], None, ALU.mult))
                for n in range(8):
                    tt, h = n // 4, n % 4
                    ns = SEQ if tt else P
                    j = 2 * (1 + h // 2) if tt else 0
                    cols = slice((h % 2) * ns, (h % 2 + 1) * ns) if tt else slice(h * ns, (h + 1) * ns)
                    c = 8 * tt + 2 * h
                    t = tmp[:, n % 2, 0:ns]
                    then(V.tensor_scalar(t, pbuf[:, j + 1, cols], psum_row[:, 2, c + 1:c + 2], None, ALU.mult))
                    p = pbuf[:, j, cols]
                    ins = V.scalar_tensor_tensor(p, p, psum_row[:, 1, c:c + 1], t, ALU.mult, ALU.add)
                    if n in (3, 5, 7):
                        ins.then_inc(diff_dve.sem, diff_dve.tick())
                for tt in range(TT):
                    b = take()
                    V.tensor_copy(yb[:, tt, :], b[:, :]).then_inc(dve_freed.sem, dve_freed.tick())
                eng.wait_ge(dve_freed.sem, dve.latest(dve_freed))
                out_norm().then_inc(yb_dve.sem, yb_dve.tick())

                eng.wait_ge(sig_act.sem, dve.next(sig_act, 2))
                for br in range(3):
                    for tt in range(TT):
                        for h in range(2):
                            b = take()
                            g = zc(tt, C_G + br * D + h * HALF, HALF)
                            m = xs[:, tt, h * HALF:(h + 1) * HALF]
                            if br == 0:
                                emptied(V.tensor_tensor(m, b[:, :], g, ALU.mult))
                            else:
                                t = tmp[:, 2 * (tt % 2) + h, :]
                                emptied(V.tensor_tensor(t, b[:, :], g, ALU.mult))
                                ins = V.tensor_tensor(m, m, t, ALU.add)
                                if br < 2:
                                    then(ins)
                ins.then_inc(mrg_dve.sem, mrg_dve.tick())
                evac_features(None)
                add_to_x()
                norm(G_FFN + 8 * li, first_lows)
                ffn_dve(groups1, True)
                add_to_x((1, 0))

            causal2 = cz[:, :]
            V.memset(cz[:, 0:P], 0.0)
            then(V.tensor_copy(cz[:, P:SEQ], const[:, K_DIAG:K_DIAG + P]))
            for li in range(DEPTH):
                layer(li)

            norm(G_MIX0)
            eng.wait_ge(late.sem, dve.next(late, 32))
            for i in range(8):
                b = take()
                t1, t2 = b[:, 0:SEQ], b[:, SEQ:HALF]
                c, s = table2[:, K_COSR:K_COSR + SEQ], table2[:, K_SINR:K_SINR + SEQ]
                u = [tmp[:, j, 0:SEQ] for j in range(4)]
                V.tensor_tensor(u[0], t1, c, ALU.mult)
                V.tensor_tensor(u[1], t2, s, ALU.mult)
                V.tensor_tensor(u[2], t1, s, ALU.mult)
                emptied(V.tensor_tensor(u[3], t2, c, ALU.mult))
                V.tensor_tensor(qT2[:, 2 * i, :], u[0], u[1], ALU.subtract)
                V.tensor_tensor(qT2[:, 2 * i + 1, :], u[2], u[3], ALU.add).then_inc(ret_dve.sem, ret_dve.tick())
                eng.wait_ge(ret_dve.sem, dve.latest(ret_dve))
            for h in range(RH):
                b = take()
                d = table2[:, K_DECAY + h * 384:K_DECAY + (h + 1) * 384]
                ins = V.tensor_tensor(pbuf[:, h, 0:384], b[:, 0:384], d, ALU.mult)
                ins.then_inc(dve_freed.sem, dve_freed.tick())
            eng.wait_ge(act_freed.sem, dve.point("ret_o", act_freed))
            mean_squares(hsum[:, 1, 0:8], hsum[:, 0, 0:8], HALF)
            then(inverse_root(hsum, slice(0, 8)))
            eng.wait_ge(rsilu_act.sem, dve.next(rsilu_act))
            for tt in range(TT):
                for h in range(RH):
                    o = rv[:, tt, h * HALF:(h + 1) * HALF]
                    ins = V.scalar_tensor_tensor(o, o, hsum[:, 3, tt * 4 + h:tt * 4 + h + 1], rg[:, tt, h * HALF:(h + 1) * HALF],
                                                 ALU.mult, ALU.mult)
            ins.then_inc(rets_dve.sem, rets_dve.tick())
            add_to_x()
            norm(G_FFN0, first_lows)
            ffn_dve(groups2, True)
            add_to_x((1, 0))

            norm(G_MIX1)
            V.memset(upad[:, :, 0:2], 0.0)
            eng.wait_ge(act_freed.sem, dve.point("conv2 C", act_freed))
            for c in range(4):
                b = take()
                ins = V.tensor_tensor(upad[:, 2 * c:2 * c + 2, 2:SEQ + 2], b[:, :].rearrange("p (f t) -> p f t", f=2),
                                      cC[:, 2 * c:2 * c + 2, :], ALU.mult)
                ins.then_inc(dve_freed.sem, dve_freed.tick())
            eng.wait_ge(dve_freed.sem, dve.latest(dve_freed))
            for f in range(KT):
                w = [gcol[:, G_CW2 + j * KT + f:G_CW2 + j * KT + f + 1] for j in range(3)]
                o = cyT[:, f, :]
                then(V.tensor_scalar(o, upad[:, f, 0:SEQ], w[0], None, ALU.mult))
                for j in (1, 2):
                    then(V.scalar_tensor_tensor(o, upad[:, f, j:j + SEQ], w[j], o, ALU.mult, ALU.add))
            eng.wait_ge(act_freed.sem, dve.point("conv2 B", act_freed))
            V.tensor_tensor(cyT, cyT, cB, ALU.mult).then_inc(conv2_dve.sem, conv2_dve.tick())
            add_to_x()

            norm(G_FFN1)
            b = take()
            r = [rt[:, i, :, :] for i in range(12)]
            emptied(V.tensor_copy(r[R_LOGIT], b[:, 0:16].rearrange("p (t e) -> p t e", t=TT)))
            tri = const[:, K_TRI:K_TRI + NE * NE].rearrange("p (a b) -> p a b", a=NE)
            for tt in range(TT):
                l = rt[:, R_LOGIT, tt, :]
                other = l.unsqueeze(1).broadcast_to([P, NE, NE])
                mine = bc(l, NE)
                c0, c1 = (cmp[:, i, :].rearrange("p (a b) -> p a b", a=NE) for i in range(2))
                V.tensor_tensor(c0, other, mine, ALU.is_gt)
                then(V.tensor_tensor(c1, other, mine, ALU.is_equal))
                then(V.tensor_tensor(c1, c1, tri, ALU.mult))
                then(V.tensor_tensor(c0, c0, c1, ALU.add))
                then(V.tensor_reduce(rt[:, R_RANK, tt, :], c0, AX.X, ALU.add))
            V.tensor_scalar(r[R_M0], r[R_RANK], 0.0, None, ALU.is_equal)
            V.tensor_scalar(r[R_M1], r[R_RANK], 1.0, None, ALU.is_equal)
            V.tensor_scalar(r[R_MASK], r[R_RANK], 2.0, None, ALU.is_lt).then_inc(mask_dve.sem, mask_dve.tick())
            eng.wait_ge(mask_dve.sem, dve.latest(mask_dve))
            for i, m in enumerate((R_M0, R_M1)):
                then(V.tensor_tensor(r[R_TMP], r[m], r[R_LOGIT], ALU.mult))
                then(V.tensor_reduce(rt2[:, i, :], r[R_TMP], AX.X, ALU.add))
            V.tensor_tensor(rt2[:, 2, :], rt2[:, 1, :], rt2[:, 0, :], ALU.subtract).then_inc(diff2_dve.sem, diff2_dve.tick())
            eng.wait_ge(exp2_act.sem, dve.next(exp2_act))
            then(V.tensor_scalar(rt2[:, 4, :], rt2[:, 3, :], 1.0, None, ALU.add))
            then(V.reciprocal(rt2[:, 4, :], rt2[:, 4, :]))
            then(V.tensor_tensor(rt2[:, 5, :], rt2[:, 3, :], rt2[:, 4, :], ALU.mult))
            then(V.tensor_tensor(r[R_GATE], r[R_M0], bc(rt2[:, 4, :], NE), ALU.mult))
            then(V.tensor_tensor(r[R_TMP], r[R_M1], bc(rt2[:, 5, :], NE), ALU.mult))
            then(V.tensor_tensor(r[R_GATE], r[R_GATE], r[R_TMP], ALU.add))
            then(V.tensor_scalar(r[R_TMP], r[R_MASK], -1000.0, 1000.0, ALU.mult, ALU.add))
            b = take()
            V.memset(route[:, :, :, NE:NE + 1], 0.0)
            V.memset(cnt[:, NE:NE + 1], 0)
            V.tensor_copy(cnt[:, 0:NE], b[:, 16:24])
            V.tensor_copy(route[:, 1, :, 0:NE], r[R_GATE])
            emptied(V.tensor_tensor(route[:, 0, :, 0:NE], b[:, 0:16].rearrange("p (t e) -> p t e", t=TT), r[R_TMP],
                                    ALU.add))

            iota = const[:, K_IOTA:K_IOTA + SEQ]

            def picks(e):
                for tt in range(TT):
                    s, g = (route[:, i, tt, bass.ds(e, 1)] for i in range(2))
                    V.tensor_scalar(pick[:, tt, :], iota, s, None, ALU.is_equal)
                    ins = V.tensor_scalar(pickg[:, tt, :], iota, s, g, ALU.is_equal, ALU.mult)
                ins.then_inc(pick_dve.sem, pick_dve.tick())

            picks(0)
            lows(G_FFN1)
            with dve.trips(NE, signals) as e:
                weights_low(1)
                b = take()
                V.tensor_copy(putT.rearrange("p s t -> p (s t)"), b[:, :]).then_inc(dve_freed.sem, dve_freed.tick())
                ffn_dve(groups2, False, lambda: picks(e + 1))
                lows(G_FFN1)
                for h in range(2):
                    b = take()
                    V.tensor_copy(ysb[:, 1, h * HALF:(h + 1) * HALF], b[:, :]).then_inc(dve_freed.sem, dve_freed.tick())
                add_to_x()

            norm_inverse()
            for tt in range(TT):
                ins = V.scalar_tensor_tensor(xs[:, tt, :], x[:, tt, :], xsum[:, 3, tt:tt + 1], fin_g[:, :], ALU.mult, ALU.mult)
            ins.then_inc(out_dve.sem, out_dve.tick())

        @block.gpsimd
        def _(eng):
            pool = Engine(eng, "pool", points)
            nth_split = [0]

            def weights_high(groups):
                first = nth_split[0]
                for i in range(len(groups) + 1):
                    up, dn = group_units(i, groups)
                    for _ in range(2 * up + dn):
                        n, m = unit_of_split[nth_split[0]], nth_split[0]
                        nth_split[0] += 1
                        arrived = loaded[n % RING]
                        eng.wait_ge(arrived.sem, pool.at(arrived, 16 * (n // RING + 1)))
                        if m - SPLITS >= first:
                            sig, value = split_read[m - SPLITS]
                            eng.wait_ge(sig.sem, pool.at(sig, value))
                        nc.gpsimd.tensor_scalar(split[:, m % SPLITS, 0, :], ring[:, n % RING, :], 1.0, 0.0, ALU.mult,
                                                ALU.add).then_inc(high_made.sem, high_made.tick())

            for groups in (groups1, groups1, groups2):
                eng.wait_ge(dve_freed.sem, pool.point("mixed", dve_freed))
                weights_high(groups)


        @block.sync
        def _(eng):
            sp = Engine(eng, "sp", points)
            n = 0

            def rows(name, lo, count, cols=P):
                return a[name][lo:lo + count, :]

            def load(dst, src):
                eng.dma_start(dst, src).then_inc(params.sem, params.tick(16))

            for name, r0, nr, t in (("norm_mix_g", G_MIX, 16, 0), ("norm_ffn_g", G_FFN, 16, 0),
                                    ("mlstm_conv_b", G_CB, 16, 0), ("mlstm_conv_w", G_CW, 64, 0),
                                    ("mlstm_norm_g", G_MN, 8, 0), ("dsa_kv_norm_g", G_KV, 4, 0),
                                    ("diff_out_norm_g", G_DO, 2, 0), ("norm_mix0_2", G_MIX0, 8, 1),
                                    ("norm_ffn0_2", G_FFN0, 8, 1), ("norm_mix1_2", G_MIX1, 8, 1),
                                    ("norm_ffn1_2", G_FFN1, 8, 1), ("conv_w_2", G_CW2, 24, 1)):
                r = r0 - (G_ROWS_A if t else 0)
                load(grow[r:r + nr, t, :], a[name + "_rows"])
            load(const[:, :], a["tables"])
            load(x[:, :, :], a["x"].rearrange("b (t p) c -> p (b t) c", p=P))
            for i, name in enumerate(("dsa_q_norm_g", "dsa_k_norm_g", "diff_q_norm_g", "diff_k_norm_g")):
                load(qk_gain[:, i, :, :], a[name].partition_broadcast(P))
            load(lamv[:, :, :, :], a["diff_lambda"].partition_broadcast(P))
            load(gateb[:, :], a["gate_b_by_head"])
            load(bgate[:, :], a["b_gate"].rearrange("l (c n) -> (l c) n", n=HALF))
            for li in range(DEPTH):
                load(w_if[:, li, :, :], a["w_in"][li, :, C_IF:C_IF + 8].rearrange("(k p) c -> p k c", p=P))
            load(w_rt[:, :, :], a["moe_router_2"].rearrange("(k p) c -> p k c", p=P))
            assert params.marked == 16 * PARAMS

            def stream(src, shape):
                nonlocal n
                if n >= RING:
                    sig, value = unit_read[n - RING]
                    if sp.trip is not None and n - RING < first_unit[0]:
                        sig, value = unit_read[n - RING + EXPERT_UNITS]
                        value -= sig.per_trip
                    eng.wait_ge(sig.sem, sp.at(sig, value))
                eng.dma_start(place(n, shape), src).then_inc(loaded[n % RING].sem, 16)
                n += 1

            def columns(w, col, width=512):
                for kh in range(2):
                    stream(unit_k(w, col, width, kh), (4, width))

            def rows_of(w, count, first=0):
                for r in range(first, first + count):
                    stream(unit_r(w, r), (2, 1024))

            def ffn_stream(groups, wg, wu, wd):
                def part(w, c, width):
                    if width == 512:
                        columns(w, c)
                    else:
                        stream(w[:, c:c + width].rearrange("(k p) c -> p k c", p=P), (8, width))
                for i in range(len(groups) + 1):
                    if i < len(groups):
                        c, width = groups[i]
                        part(wg, c, width)
                        part(wu, c, width)
                    if i:
                        c, width = groups[i - 1]
                        rows_of(wd, width // 256, c // 256)

            for li in range(DEPTH):
                w_in = a["w_in"][li]
                gates = list(g_chunks)

                def gate_columns(m):
                    for _ in range(m):
                        columns(w_in, gates.pop(0)[0])

                columns(w_in, C_QK)
                columns(w_in, C_QK + 512)
                for col, width in z_chunks:
                    columns(w_in, col, width)
                gate_columns(gates_after["z"])
                rows_of(a["dsa_w_kv_up"][li], 1)
                gate_columns(gates_after["kv"])
                gate_columns(gates_after["mlstm"])
                gate_columns(gates_after["dsa"])
                gate_columns(gates_after["diff"])
                gate_columns(len(gates))
                for br in range(3):
                    rows_of(a["w_branch"][li, br], 2)
                rows_of(a["w_out"][li], 4)
                wgu = a["w_gate_up"][li]
                ffn_stream(groups1, wgu[:, 0:FF1], wgu[:, FF1:2 * FF1], a["w_down"][li])
            eng.wait_ge(mrg_dve.sem, sp.at(mrg_dve, DEPTH))
            eng.dma_start(table2, a["tables2"]).then_inc(late.sem, late.tick(16))
            eng.dma_start(fin_g, a["norm_final_2"].partition_broadcast(P)).then_inc(late.sem, late.tick(16))
            for c in range(12):
                columns(a["ret_w_in_2"], 512 * c)
            rows_of(a["ret_w_out_2"], 8)
            ffn_stream(groups2, a["ffn_w_gate_2"], a["ffn_w_up_2"], a["ffn_w_down_2"])
            for c in (2, 3, 4, 5, 0, 1):
                columns(a["conv_w_in_2"], 512 * c)
            rows_of(a["conv_w_out_2"], 4)
            for i in range(n - RING, n):
                eng.wait_ge(unit_read[i][0].sem, unit_read[i][1])
            first_unit = [n]
            with sp.trips(NE, signals) as e:
                def of(w):
                    return a[w][bass.ds(e, 1)].rearrange("e k c -> (e k) c")
                ffn_stream(groups2, of("moe_w_gate_2"), of("moe_w_up_2"), of("moe_w_down_2"))
                assert n - first_unit[0] == EXPERT_UNITS
            eng.wait_ge(out_dve.sem, sp.next(out_dve))
            eng.dma_start(out.rearrange("b (t p) c -> p (b t) c", p=P), xs[:, :, :]).then_inc(stored.sem, stored.tick(16))
            eng.wait_ge(stored.sem, sp.next(stored, 16))


def tables():
    t = np.zeros((P, K_COLS), np.float32)
    t2 = np.zeros((P, K2_COLS), np.float32)
    f = np.float32
    pos = np.arange(SEQ, dtype=f)
    inv = (1.0 / np.power(f(10000.0), np.arange(0, HD, 2, dtype=f) / f(HD))).astype(f)
    ang = (pos[:, None] * inv[None, :]).astype(f)
    c, s = np.cos(ang), np.sin(ang)
    for tt in range(TT):
        r = slice(tt * P, (tt + 1) * P)
        t[:, K_C2 + tt * HD:K_C2 + (tt + 1) * HD] = np.concatenate([c[r], c[r]], 1)
        t[:, K_S2 + tt * HD:K_S2 + (tt + 1) * HD] = np.concatenate([-s[r], s[r]], 1)
    inv = np.power(f(10000.0), -np.arange(0, 256, 2, dtype=f) / f(256)).astype(f)
    ang = (inv[:, None] * pos[None, :]).astype(f)
    t2[:, K_COSR:K_COSR + SEQ], t2[:, K_SINR:K_SINR + SEQ] = np.cos(ang), np.sin(ang)
    row, col = np.arange(P)[:, None], np.arange(P)[None, :]
    for h in range(RH):
        log_gamma = np.log(1.0 - 2.0 ** (-5.0 - h))
        for o, key0, q0, n in ((0, 0, 0, SEQ), (SEQ, P, P, P)):
            d = (q0 + np.arange(n))[None, :] - (key0 + np.arange(P))[:, None]
            t2[:, K_DECAY + h * 384 + o:K_DECAY + h * 384 + o + n] = np.where(
                d >= 0, np.exp(np.maximum(d, 0) * log_gamma), 0.0) * 256 ** -0.5
    t[:, K_ID:K_ID + P] = np.eye(P)
    t[:, K_DIAG:K_DIAG + P] = np.where(col <= row, 0.0, NEG)
    t[:, K_CMT:K_CMT + P] = np.where(row <= col, 0.0, NEG)
    t[:, K_CMT + SEQ:K_CMT + 384] = t[:, K_CMT:K_CMT + P]
    t[:, K_UT:K_UT + P] = row < col
    t[:, K_ONE:K_ONE + P] = 1.0
    t[:, K_IOTA:K_IOTA + SEQ] = np.arange(SEQ)
    e = np.arange(NE)
    t[:, K_TRI:] = (e[None, :] < e[:, None]).astype(f).reshape(1, -1)
    return t, t2


ROWS = ("norm_mix_g", "norm_ffn_g", "mlstm_conv_b", "mlstm_conv_w", "mlstm_norm_g", "dsa_kv_norm_g",
        "diff_out_norm_g", "norm_mix0_2", "norm_ffn0_2", "norm_mix1_2", "norm_ffn1_2", "conv_w_2")
OTHER = ("x", "w_in", "b_gate", "dsa_w_kv_up", "dsa_q_norm_g", "dsa_k_norm_g",
         "diff_q_norm_g", "diff_k_norm_g", "diff_lambda", "w_branch", "w_out", "w_gate_up", "w_down",
         "ret_w_in_2", "ret_w_out_2", "ffn_w_gate_2", "ffn_w_up_2", "ffn_w_down_2", "conv_w_in_2",
         "conv_w_out_2", "moe_router_2", "moe_w_gate_2", "moe_w_up_2", "moe_w_down_2", "norm_final_2")


def kernel(**inputs):
    import concourse.bacc as bacc
    from concourse.bass_utils import run_bass_kernel_spmd

    nc = bacc.Bacc("TRN2", target_bir_lowering=False, num_devices=1)
    arrays = {name: np.ascontiguousarray(inputs[name]) for name in OTHER}
    arrays |= {name + "_rows": np.ascontiguousarray(inputs[name]).reshape(-1, P) for name in ROWS}
    gate_b = np.asarray(inputs["mlstm_gate_b"]).reshape(2 * DEPTH, M_HEADS)
    arrays["gate_b_by_head"] = np.ascontiguousarray(gate_b.T)
    arrays["tables"], arrays["tables2"] = tables()
    aps = {name: nc.dram_tensor("in_" + name, v.shape, mybir.dt.from_np(v.dtype), kind="ExternalInput").ap()
           for name, v in arrays.items()}
    out = nc.dram_tensor("out", (1, SEQ, D), F32, kind="ExternalOutput").ap()
    build(nc, aps, out)
    r = run_bass_kernel_spmd(nc, [{"in_" + k: v for k, v in arrays.items()}], core_ids=[0])
    return r.results[0]["out"]
```
